# Optimizing a Trainium2 kernel written in Bass

```python
import math
import jax, jax.numpy as jnp
from jax import lax
import numpy as np

D_MODEL = 1024
BATCH = 1
SEQ = 512
DEPTH = 2
DEC_BATCH = 8
DEC_SEQ = 16
PAST_LEN = 256

CHUNK = 64
N_A_LAYERS = DEPTH // 2
N_B_LAYERS = DEPTH - N_A_LAYERS
MLSTM_INNER = 2 * D_MODEL
MLSTM_HEADS = 4
MLSTM_HEAD_DIM = MLSTM_INNER // MLSTM_HEADS
QKV_BLOCK = 4
CONV_WIDTH = 4
MLA_HEADS = 8
QK_NOPE_DIM = 128
QK_ROPE_DIM = 64
V_HEAD_DIM = 128
KV_LORA_RANK = 256
Q_LORA_RANK = 384
MLA_GATE_WIDTH = MLA_HEADS * V_HEAD_DIM
MLA_SCALE = 1.0 / math.sqrt(QK_NOPE_DIM + QK_ROPE_DIM)
ROPE_BASE = 10000.0
Q_BLOCK = 128
EPS = 1e-6

kernel_name = "yoco_mlstm_mla_stream_step"

def rmsnorm(x, w):
    xf = x.astype(jnp.float32)
    y = xf * lax.rsqrt(jnp.mean(xf * xf, axis=-1, keepdims=True) + EPS)
    return (y * w.astype(jnp.float32)).astype(x.dtype)

def rope(x, pos):
    half = x.shape[-1] // 2
    inv = ROPE_BASE ** (-jnp.arange(half, dtype=jnp.float32) / half)
    ang = pos.astype(jnp.float32)[:, None] * inv[None, :]
    cos = jnp.cos(ang)[None, :, None, :]
    sin = jnp.sin(ang)[None, :, None, :]
    xf = x.astype(jnp.float32)
    x1, x2 = xf[..., :half], xf[..., half:]
    return jnp.concatenate([x1 * cos - x2 * sin, x1 * sin + x2 * cos], axis=-1).astype(x.dtype)

def causal_conv(x, buf, w, b):
    T = x.shape[1]
    xp = jnp.concatenate([buf.astype(x.dtype), x], axis=1)
    y = b + xp[:, 0:T] * w[0]
    for j in range(1, CONV_WIDTH):
        y = y + xp[:, j:j + T] * w[j]
    return y, xp[:, xp.shape[1] - (CONV_WIDTH - 1):]

def headwise(x, w):
    B, T, _ = x.shape
    xb = x.reshape(B, T, -1, QKV_BLOCK)
    return jnp.einsum('btgi,gio->btgo', xb, w).reshape(B, T, -1)

def mlstm_chunk_step(carry, blk):
    C, n, m = carry
    q, k, v, ig, lf = blk
    L = q.shape[2]
    b = jnp.cumsum(lf, axis=-1)
    causal = jnp.tril(jnp.ones((L, L), dtype=bool))
    d_log = jnp.where(causal, b[..., :, None] - b[..., None, :] + ig[..., None, :], -jnp.inf)
    inter_log = b + m[..., None]
    m_t = jnp.maximum(inter_log, jnp.max(d_log, axis=-1))
    w_intra = jnp.exp(d_log - m_t[..., None])
    w_inter = jnp.exp(inter_log - m_t)
    s = jnp.einsum('bhtd,bhsd->bhts', q, k) * w_intra
    num = w_inter[..., None] * jnp.einsum('bhvk,bhtk->bhtv', C, q) + jnp.einsum('bhts,bhsv->bhtv', s, v)
    den = w_inter * jnp.einsum('bhk,bhtk->bht', n, q) + jnp.sum(s, axis=-1)
    h = num / jnp.maximum(jnp.abs(den), jnp.exp(-m_t))[..., None]
    b_last = b[..., -1]
    w_log = b_last[..., None] - b + ig
    m_new = jnp.maximum(b_last + m, jnp.max(w_log, axis=-1))
    decay = jnp.exp(b_last + m - m_new)
    w_upd = jnp.exp(w_log - m_new[..., None])
    C_new = decay[..., None, None] * C + jnp.einsum('bhsv,bhsk->bhvk', v * w_upd[..., None], k)
    n_new = decay[..., None] * n + jnp.einsum('bhs,bhsk->bhk', w_upd, k)
    return (C_new, n_new, m_new), h

def mlstm_scan(q, k, v, ig, lf, C0, n0, m0):
    B, H, T, d = q.shape
    L = min(CHUNK, T)
    nc = T // L

    def blocks(a):
        return jnp.moveaxis(a.reshape(a.shape[:2] + (nc, L) + a.shape[3:]), 2, 0)

    (C, n, m), h = lax.scan(mlstm_chunk_step, (C0, n0, m0), (blocks(q), blocks(k), blocks(v), blocks(ig), blocks(lf)))
    h = jnp.moveaxis(h, 0, 2).reshape(B, H, T, d)
    return h, C, n, m

def mlstm_layer(x, C0, n0, m0, buf, norm_w, w_in, conv_w, conv_b, w_q, w_k, w_v, w_gates, b_gates, outnorm_w, skip, w_out):
    B, T, _ = x.shape
    H, d = MLSTM_HEADS, MLSTM_HEAD_DIM
    u = rmsnorm(x, norm_w) @ w_in
    x_in, z = u[..., :MLSTM_INNER], u[..., MLSTM_INNER:]
    xc_pre, new_buf = causal_conv(x_in, buf, conv_w, conv_b)
    xc = jax.nn.silu(xc_pre)
    q = headwise(xc, w_q)
    k = headwise(xc, w_k)
    v = headwise(x_in, w_v)
    g = (q @ w_gates[:MLSTM_INNER] + k @ w_gates[MLSTM_INNER:2 * MLSTM_INNER]
         + v @ w_gates[2 * MLSTM_INNER:] + b_gates).astype(jnp.float32)
    ig = jnp.transpose(g[..., :H], (0, 2, 1))
    lf = jnp.transpose(jax.nn.log_sigmoid(g[..., H:]), (0, 2, 1))

    def heads(a):
        return jnp.transpose(a.astype(jnp.float32).reshape(B, T, H, d), (0, 2, 1, 3))

    h, C, n, m = mlstm_scan(heads(q), heads(k) / math.sqrt(d), heads(v), ig, lf,
                            C0.astype(jnp.float32), n0.astype(jnp.float32), m0.astype(jnp.float32))
    mu = jnp.mean(h, axis=-1, keepdims=True)
    var = jnp.mean(jnp.square(h - mu), axis=-1, keepdims=True)
    hn = (h - mu) * lax.rsqrt(var + EPS)
    hn = jnp.transpose(hn, (0, 2, 1, 3)).reshape(B, T, MLSTM_INNER) * outnorm_w.astype(jnp.float32)
    y = (hn.astype(x.dtype) + skip * xc) * jax.nn.silu(z)
    return x + y @ w_out, C, n, m, new_buf

def shared_latent_kv(s, pos, kv_norm_w, kv_w_dkv, kv_latent_norm_w):
    u = rmsnorm(s, kv_norm_w) @ kv_w_dkv
    c_kv = rmsnorm(u[..., :KV_LORA_RANK], kv_latent_norm_w)
    k_pe = rope(u[..., None, KV_LORA_RANK:], pos)[:, :, 0]
    return c_kv, k_pe

def mla_block_attend(q_lat, q_pe, q_pos, c_kv, k_pe, k_pos):
    s = (jnp.einsum('bthr,bsr->bhts', q_lat, c_kv) + jnp.einsum('bthp,bsp->bhts', q_pe, k_pe)).astype(jnp.float32) * MLA_SCALE
    visible = (k_pos[None, :] // CHUNK) <= (q_pos[:, None] // CHUNK)
    s = jnp.where(visible[None, None], s, -jnp.inf)
    p = jax.nn.softmax(s, axis=-1).astype(c_kv.dtype)
    return jnp.einsum('bhts,bsr->bthr', p, c_kv)

def mla_attend(q_lat, q_pe, q_pos, c_kv, k_pe, k_pos):
    B, T = q_lat.shape[:2]
    if T > Q_BLOCK and T % Q_BLOCK == 0:
        nb = T // Q_BLOCK

        def split(a):
            return jnp.moveaxis(a.reshape((B, nb, Q_BLOCK) + a.shape[2:]), 1, 0)

        o = lax.map(lambda blk: mla_block_attend(blk[0], blk[1], blk[2], c_kv, k_pe, k_pos),
                    (split(q_lat), split(q_pe), q_pos.reshape(nb, Q_BLOCK)))
        return jnp.moveaxis(o, 0, 1).reshape((B, T) + o.shape[3:])
    return mla_block_attend(q_lat, q_pe, q_pos, c_kv, k_pe, k_pos)

def mla_layer(x, q_pos, c_kv, k_pe, k_pos, norm_w, w_in, q_norm_w, w_uq, w_out, kv_w_uk, kv_w_uv):
    B, T, _ = x.shape
    u = rmsnorm(x, norm_w) @ w_in
    cq = rmsnorm(u[..., :Q_LORA_RANK], q_norm_w)
    gate = u[..., Q_LORA_RANK:]
    q = (cq @ w_uq).reshape(B, T, MLA_HEADS, QK_NOPE_DIM + QK_ROPE_DIM)
    q_nope = q[..., :QK_NOPE_DIM]
    q_pe = rope(q[..., QK_NOPE_DIM:], q_pos)
    q_lat = jnp.einsum('bthn,rhn->bthr', q_nope, kv_w_uk)
    o_lat = mla_attend(q_lat, q_pe, q_pos, c_kv, k_pe, k_pos)
    o = jnp.einsum('bthr,rhv->bthv', o_lat, kv_w_uv).reshape(B, T, MLA_GATE_WIDTH)
    return x + (o * jax.nn.silu(gate)) @ w_out

def trunk(x, pos, C0, n0, m0, buf0, past_ckv, past_kpe,
          a_norm_w, a_w_in, a_conv_w, a_conv_b, a_w_q, a_w_k, a_w_v, a_w_gates, a_b_gates, a_outnorm_w, a_skip, a_w_out,
          kv_norm_w, kv_w_dkv, kv_latent_norm_w, kv_w_uk, kv_w_uv,
          b_norm_w, b_w_in, b_q_norm_w, b_w_uq, b_w_out, final_norm_w):
    new_C, new_n, new_m, new_buf = [], [], [], []
    c_kv = k_pe = keys_ckv = keys_kpe = k_pos = None
    for layer in range(DEPTH):
        if layer < N_A_LAYERS:
            l = layer
            x, C, n, m, buf = mlstm_layer(x, C0[l], n0[l], m0[l], buf0[l], a_norm_w[l], a_w_in[l], a_conv_w[l], a_conv_b[l],
                                          a_w_q[l], a_w_k[l], a_w_v[l], a_w_gates[l], a_b_gates[l], a_outnorm_w[l], a_skip[l], a_w_out[l])
            new_C.append(C)
            new_n.append(n)
            new_m.append(m)
            new_buf.append(buf)
            if layer == N_A_LAYERS - 1:
                c_kv, k_pe = shared_latent_kv(x, pos, kv_norm_w, kv_w_dkv, kv_latent_norm_w)
                keys_ckv = jnp.concatenate([past_ckv.astype(c_kv.dtype), c_kv], axis=1)
                keys_kpe = jnp.concatenate([past_kpe.astype(k_pe.dtype), k_pe], axis=1)
                k_pos = jnp.concatenate([jnp.arange(past_ckv.shape[1], dtype=jnp.int32), pos])
        else:
            l = layer - N_A_LAYERS
            x = mla_layer(x, pos, keys_ckv, keys_kpe, k_pos, b_norm_w[l], b_w_in[l], b_q_norm_w[l], b_w_uq[l], b_w_out[l],
                          kv_w_uk, kv_w_uv)
    y = rmsnorm(x, final_norm_w)
    return y, jnp.stack(new_C), jnp.stack(new_n), jnp.stack(new_m), jnp.stack(new_buf), c_kv, k_pe

def setup_inputs(seed: int = 0) -> dict:
    key = jax.random.key(seed)
    ks = jax.random.split(key, 40)
    f32 = jnp.float32
    nrm = lambda i, shape, scale: scale * jax.random.normal(ks[i], shape, f32)
    H, d = MLSTM_HEADS, MLSTM_HEAD_DIM
    return {
        "x_prompt": nrm(0, (BATCH, SEQ, D_MODEL), 1.0),
        "x_sample": nrm(1, (DEC_BATCH, DEC_SEQ, D_MODEL), 1.0),
        "state_mlstm_C": nrm(2, (N_A_LAYERS, DEC_BATCH, H, d, d), 0.05),
        "state_mlstm_n": nrm(3, (N_A_LAYERS, DEC_BATCH, H, d), 0.05),
        "state_mlstm_m": nrm(4, (N_A_LAYERS, DEC_BATCH, H), 0.5),
        "state_mlstm_conv": nrm(5, (N_A_LAYERS, DEC_BATCH, CONV_WIDTH - 1, MLSTM_INNER), 1.0),
        "cache_mla_ckv": nrm(6, (DEC_BATCH, PAST_LEN, KV_LORA_RANK), 1.0),
        "cache_mla_kpe": nrm(7, (DEC_BATCH, PAST_LEN, QK_ROPE_DIM), 1.0),
        "a_norm_w": 1.0 + nrm(8, (N_A_LAYERS, D_MODEL), 0.02),
        "a_w_in": nrm(9, (N_A_LAYERS, D_MODEL, 2 * MLSTM_INNER), D_MODEL ** -0.5),
        "a_conv_w": nrm(10, (N_A_LAYERS, CONV_WIDTH, MLSTM_INNER), CONV_WIDTH ** -0.5),
        "a_conv_b": nrm(11, (N_A_LAYERS, MLSTM_INNER), 0.02),
        "a_w_q": nrm(12, (N_A_LAYERS, MLSTM_INNER // QKV_BLOCK, QKV_BLOCK, QKV_BLOCK), QKV_BLOCK ** -0.5),
        "a_w_k": nrm(13, (N_A_LAYERS, MLSTM_INNER // QKV_BLOCK, QKV_BLOCK, QKV_BLOCK), QKV_BLOCK ** -0.5),
        "a_w_v": nrm(14, (N_A_LAYERS, MLSTM_INNER // QKV_BLOCK, QKV_BLOCK, QKV_BLOCK), QKV_BLOCK ** -0.5),
        "a_w_gates": nrm(15, (N_A_LAYERS, 3 * MLSTM_INNER, 2 * H), (3 * MLSTM_INNER) ** -0.5),
        "a_b_gates": jnp.concatenate([nrm(16, (N_A_LAYERS, H), 0.1),
                                      jax.random.uniform(ks[17], (N_A_LAYERS, H), f32, 3.0, 6.0)], axis=-1),
        "a_outnorm_w": 1.0 + nrm(18, (N_A_LAYERS, MLSTM_INNER), 0.02),
        "a_skip": 1.0 + nrm(19, (N_A_LAYERS, MLSTM_INNER), 0.02),
        "a_w_out": nrm(20, (N_A_LAYERS, MLSTM_INNER, D_MODEL), MLSTM_INNER ** -0.5),
        "kv_norm_w": 1.0 + nrm(21, (D_MODEL,), 0.02),
        "kv_w_dkv": nrm(22, (D_MODEL, KV_LORA_RANK + QK_ROPE_DIM), D_MODEL ** -0.5),
        "kv_latent_norm_w": 1.0 + nrm(23, (KV_LORA_RANK,), 0.02),
        "kv_w_uk": nrm(24, (KV_LORA_RANK, MLA_HEADS, QK_NOPE_DIM), KV_LORA_RANK ** -0.5),
        "kv_w_uv": nrm(25, (KV_LORA_RANK, MLA_HEADS, V_HEAD_DIM), KV_LORA_RANK ** -0.5),
        "b_norm_w": 1.0 + nrm(26, (N_B_LAYERS, D_MODEL), 0.02),
        "b_w_in": nrm(27, (N_B_LAYERS, D_MODEL, Q_LORA_RANK + MLA_GATE_WIDTH), D_MODEL ** -0.5),
        "b_q_norm_w": 1.0 + nrm(28, (N_B_LAYERS, Q_LORA_RANK), 0.02),
        "b_w_uq": nrm(29, (N_B_LAYERS, Q_LORA_RANK, MLA_HEADS * (QK_NOPE_DIM + QK_ROPE_DIM)), Q_LORA_RANK ** -0.5),
        "b_w_out": nrm(30, (N_B_LAYERS, MLA_GATE_WIDTH, D_MODEL), MLA_GATE_WIDTH ** -0.5),
        "final_norm_w": 1.0 + nrm(31, (D_MODEL,), 0.02),
    }

def reference(x_prompt, x_sample, state_mlstm_C, state_mlstm_n, state_mlstm_m, state_mlstm_conv, cache_mla_ckv, cache_mla_kpe,
              a_norm_w, a_w_in, a_conv_w, a_conv_b, a_w_q, a_w_k, a_w_v, a_w_gates, a_b_gates, a_outnorm_w, a_skip, a_w_out,
              kv_norm_w, kv_w_dkv, kv_latent_norm_w, kv_w_uk, kv_w_uv,
              b_norm_w, b_w_in, b_q_norm_w, b_w_uq, b_w_out, final_norm_w):
    weights = (a_norm_w, a_w_in, a_conv_w, a_conv_b, a_w_q, a_w_k, a_w_v, a_w_gates, a_b_gates, a_outnorm_w, a_skip, a_w_out,
               kv_norm_w, kv_w_dkv, kv_latent_norm_w, kv_w_uk, kv_w_uv,
               b_norm_w, b_w_in, b_q_norm_w, b_w_uq, b_w_out, final_norm_w)
    H, d = MLSTM_HEADS, MLSTM_HEAD_DIM
    Bp, Tp = x_prompt.shape[0], x_prompt.shape[1]
    pos_p = jnp.arange(Tp, dtype=jnp.int32)
    y_prompt, p_C, p_n, p_m, p_conv, p_ckv, p_kpe = trunk(
        x_prompt, pos_p,
        jnp.zeros((N_A_LAYERS, Bp, H, d, d), jnp.float32),
        jnp.zeros((N_A_LAYERS, Bp, H, d), jnp.float32),
        jnp.zeros((N_A_LAYERS, Bp, H), jnp.float32),
        jnp.zeros((N_A_LAYERS, Bp, CONV_WIDTH - 1, MLSTM_INNER), x_prompt.dtype),
        jnp.zeros((Bp, 0, KV_LORA_RANK), x_prompt.dtype),
        jnp.zeros((Bp, 0, QK_ROPE_DIM), x_prompt.dtype),
        *weights)
    past_len = cache_mla_ckv.shape[1]
    pos_s = past_len + jnp.arange(x_sample.shape[1], dtype=jnp.int32)
    y_sample, s_C, s_n, s_m, s_conv, s_ckv, s_kpe = trunk(
        x_sample, pos_s, state_mlstm_C, state_mlstm_n, state_mlstm_m, state_mlstm_conv,
        cache_mla_ckv, cache_mla_kpe, *weights)
    return (y_prompt, y_sample, p_C, p_n, p_m, p_conv, p_ckv, p_kpe, s_C, s_n, s_m, s_conv, s_ckv, s_kpe)


_drawn_inputs = setup_inputs


def setup_inputs(seed=0):
    import zlib

    import numpy as np

    out = dict(_drawn_inputs(seed))
    spreads = {}
    factors = {'a_outnorm_w': 5.814,
     'a_skip': 8.0,
     'kv_norm_w': 2.692,
     'kv_latent_norm_w': 2.729,
     'b_norm_w': 8.0,
     'b_q_norm_w': 8.0,
     'final_norm_w': 2.896}
    for name, (base, spread) in spreads.items():
        noise = np.random.default_rng([zlib.crc32(name.encode()), seed]).standard_normal(out[name].shape)
        drawn = base * np.exp(spread * noise) if base else spread * noise
        out[name] = __import__('jax').numpy.asarray(drawn.astype(out[name].dtype))
    for name, factor in factors.items():
        out[name] = (out[name] * factor).astype(out[name].dtype)
    return out
```

```python
import math
from contextlib import ExitStack

import concourse.bass as bass
from concourse import mybir

F32 = mybir.dt.float32
BF16 = mybir.dt.bfloat16
ACT = mybir.ActivationFunctionType
ALU = mybir.AluOpType
AX_X = mybir.AxisListType.X

P = 128
SEQ, STREAMS, STEP, PAST = 512, 8, 16, 256
T = SEQ + STREAMS * STEP
TT = T // P
NP = SEQ // P
HALF = T // 2
D = 1024
KD = D // P
INNER = 2 * D
NI = INNER // P
HEADS, HD = 4, 512
KH = HD // P
TAPS = 4
HIST = TAPS - 1
PROMPT_X = HIST + SEQ
XPW = PROMPT_X + STREAMS * (HIST + STEP)
G8 = 2 * HEADS
VG = P + G8
LAT, ROPE, QLORA = 256, 64, 384
RT, QT = LAT // P, QLORA // P
AH = 8
PAIRS = AH // 2
EPS = 1e-6
KSCALE = float(HD) ** -0.5
ASCALE = float(128 + ROPE) ** -0.5
FAR = -1e30
SLOTS = 4
CS = 4
COMBOS = [(1, 1), (1, 2), (2, 1), (2, 2), (1, 3), (3, 1), (2, 3), (3, 2)]
V_CONV = 0
V_CB = V_CONV + NI * TAPS
V_ON = V_CB + NI
V_SK = V_ON + NI
V_AN = V_SK + NI
V_KN = V_AN + KD
V_BN = V_KN + KD
V_FN = V_BN + KD
V_LN = V_FN + KD
V_QN = V_LN + RT
V_N = V_QN + QT
R_BI, R_BF, R_M0 = 0, 1, 2
R_KEEP = R_M0 + 1 + STREAMS
R_RESET = R_KEEP + T
R_ONEH = R_RESET + T
R_N = R_ONEH + HEADS
ARENA = 36900
OFF = [0, 512, 896, 1152, 1280]
WID = [512, 384, 256, 128, 128]
DW = 1408
S_DEN, S_NQ, S_NS, S_NP = 0, 8, 16, 48


class Tally:

    def __init__(self, sem, step):
        self.sem, self.step, self.base, self.k, self.j, self.per = sem, step, 0, 0, None, 0

    def value(self, ahead=0):
        here = (self.base + self.k + ahead) * self.step
        return here if self.j is None else self.j * (self.per * self.step) + here


class Counts:

    def __init__(self, eng):
        self.eng, self.of = eng, {}

    def tally(self, sem, step=1):
        key = str(sem)
        if key not in self.of:
            self.of[key] = Tally(sem, step)
        return self.of[key]

    def up(self, sem, step=1):
        self.tally(sem, step).k += 1
        return step

    def skip(self, sem, n=1, step=1):
        self.tally(sem, step).k += n

    def all(self, sem, ahead=0, step=1):
        t = self.tally(sem, step)
        v = t.value(ahead)
        return v if t.j is not None or v > 0 else None

    def next(self, sem, step=1):
        v = self.all(sem, 1, step)
        self.skip(sem, 1, step)
        return v

    def rounds(self, times, body):
        for t in self.of.values():
            t.base, t.k = t.base + t.k, 0
        body(0)
        for t in self.of.values():
            t.per, t.k = t.k, 0
        with self.eng.Fori(1, times) as j:
            for t in self.of.values():
                t.j = j
            body(j)
            for t in self.of.values():
                assert t.k == t.per, (t.sem, t.k, t.per)
        for t in self.of.values():
            t.base, t.k, t.j = t.base + times * t.per, 0, None


def program(nc, i, o):
    with ExitStack() as ctx:
        def sem(name):
            return ctx.enter_context(nc.semaphore(name))

        def pb(name, cols):
            return ctx.enter_context(nc.psum_tensor(name, [P, cols], F32))

        v_dram = nc.dram_tensor("v_scratch", [NI, P, T], F32, kind="Internal").ap()
        k_dram = nc.dram_tensor("k_scratch", [NI, P, T], F32, kind="Internal").ap()
        z_dram = nc.dram_tensor("z_scratch", [NI, P, T], F32, kind="Internal").ap()
        kp_dram = nc.dram_tensor("k_parts", [3, P, HD], BF16, kind="Internal").ap()
        vp_dram = nc.dram_tensor("v_parts", [3, P, HD], BF16, kind="Internal").ap()

        work = [pb("work_a", 1024), pb("work_b", 1024)]
        bank = [pb(f"bank_{n}", 512) for n in range(4)]
        small = work[1][:, 512:1024]

        def halves(buf):
            return buf[:, :].rearrange("p (a b) -> p a b", a=2)[:, :, 0:HALF]

        def two(ap):
            return ap.rearrange("p (a b) -> p a b", a=2)

        def sb(name, shape, dt=F32):
            return ctx.enter_context(nc.sbuf_tensor(name, shape, dt))

        ident = sb("ident", [P, P])
        ones_f = sb("ones_f", [P, P])
        vec = sb("vec", [P, V_N])
        eps_t = sb("eps_t", [P, 1])
        ring = sb("ring", [P, SLOTS, KD, P])
        rstd = sb("rstd", [P, T])
        xc = sb("xc", [P, NI, T])
        wq_c = sb("wq_c", [P, NI + KH, 4])
        wk_c = sb("wk_c", [P, NI + KH, 4])
        bdmask = sb("bdmask", [P, 32, 4])
        gacc = sb("gacc", [P, TT, G8])
        tails = sb("tails", [P, NI, 1 + STREAMS, HIST])
        arena = sb("arena", [P, ARENA])
        top, area = [0], [arena[:, :]]

        def shaped(view, dims):
            names = "abcde"[:len(dims)]
            return view if len(dims) == 1 else view.rearrange(f"p ({' '.join(names)}) -> p {' '.join(names)}",
                                                              **dict(zip(names, dims)))

        def cut(n):
            top[0] += n
            assert top[0] <= area[0].shape[1], top[0]
            return area[0][:, top[0] - n:top[0]]

        def take(*dims):
            return shaped(cut(math.prod(dims)), dims)

        def take16(*dims):
            return shaped(cut(math.prod(dims) // 2).bitcast(BF16), dims)

        class Buffers:

            def __init__(self, stage, fill, free, bfill, bfree):
                def raised(what, which):
                    return {n: sem(f"{stage}_{what}_{n}") for n in which}

                self.fill, self.free = raised("work_filled", fill), raised("work_emptied", free)
                self.bfill, self.bfree = raised("bank_filled", bfill), raised("bank_emptied", bfree)

        A = Buffers("A", (0, 1), (0,), (0, 2), (0, 2))
        G = Buffers("G", (0, 1), (), (0, 1, 2, 3), (0,))
        B = Buffers("B", (0, 1), (0, 1), range(4), range(4))
        C = Buffers("C", (0, 1), (0, 1), (), ())
        Dd = Buffers("D", (0, 1), (0, 1), (0,), ())
        E = Buffers("E", (0, 1), (0, 1), range(4), range(4))
        F = Buffers("F", (0, 1), (0, 1), range(4), range(4))
        H = Buffers("H", (0, 1), (0, 1), (0, 1, 2), (0, 1))
        names = """const_in ones_ready squares root normed tap0 conv_done xcs_ready xc_kept tail_kept
            vs_ready ks_ready zs_ready stage_left softplus exp_args exp_rows sel_ready cols_ready misc_in
            hk_in hv_in hz_in parts_ready parts_out stack_in bd_ready qm_ready kw_ready kwsum_ready
            dmax_ready var_ready pow_ready y_ready out_done late_in pair_in lat_ready kpe_ready
            qz_ready pair_done max_ready 
            prob_ready qb_ready tok_ready y_out dve_own act_own pool_own 
            x1_in basis_ready rope_mm""".split()
        (const_in, ones_ready, squares, root, normed, tap0, conv_done, xcs_ready, xc_kept, tail_kept,
         vs_ready, ks_ready, zs_ready, stage_left, softplus, exp_args, exp_rows, sel_ready, cols_ready, misc_in,
         hk_in, hv_in, hz_in, parts_ready, parts_out, stack_in, bd_ready, qm_ready, kw_ready, kwsum_ready,
         dmax_ready, var_ready, pow_ready, y_ready, out_done, late_in, pair_in, lat_ready, kpe_ready,
         qz_ready, pair_done, max_ready,
         prob_ready, qb_ready, tok_ready, y_out, dve_own, act_own, pool_own,
         x1_in, basis_ready, rope_mm) = (sem(n) for n in names)
        x_in = [sem(f"x_in{n}") for n in range(4)]
        w_in = [sem(f"weights_in{n}") for n in range(SLOTS)]
        v_out, k_out, z_out, cp_out, keys_in = ([sem(f"{n}{s}") for s in range(2)] for n in
                                                ("v_out", "k_out", "z_out", "prompt_c_out", "keys_in"))
        c_in = [sem(f"c_in{n}") for n in range(CS)]
        c_out = [sem(f"c_out{n}") for n in range(CS)]

        block = ctx.enter_context(nc.Block())

        x_a = take(KD, T)
        xn = take(KD, T)
        hist = take(NI, STREAMS, HIST)
        wv_c = take(NI, 4)
        gqkv = take(3, NI, 4, G8)
        gprod = take(3, NI, 4, G8)
        basis = take(2, NI, VG)
        xin = [take(XPW) for _ in range(2)]
        xst = [take(P) for _ in range(2)]
        acc = [take(T) for _ in range(2)]
        xcs = [take(T) for _ in range(2)]
        vs = [take(TT, P) for _ in range(2)]
        ks = [take(TT, P) for _ in range(2)]
        zs = [take(T) for _ in range(2)]

        top[0] = 0
        ct = [take(KH, HD) for _ in range(CS)]
        kh = take(KH, TT, P)
        vh = take(KH, TT, P)
        zh = take(KH, T)
        q_t = take(KH, T)
        k_t = take(KH, T)
        h_t = k_t
        pt = take(DW)
        k_stack = take16(STREAMS, HD)
        v_stack = take16(STREAMS, HD)
        k_part = take16(3, HD)
        v_part = take16(3, HD)
        rest = take(HD)
        qm = take(KH, 2, P)
        wpar = take(2, P)
        hn = take(HD)
        bdq = take(KH, P)
        bdk = take(KH, P)
        cps = [take(HD) for _ in range(2)]
        kwsum = take(KH, P)
        st6, mv = take(6), take(2)
        tiny = take(16)
        half_neg = take(1)
        nqm = take(STREAMS)
        head_on = take(KH)
        rowc = take(R_N)
        m_row = take(T)
        wi_row = take(P)
        msel = take(T)
        wisel = take(P)
        decsel = take(HEADS, STREAMS)
        decb = take(HEADS, STREAMS)
        cols = take(3, TT, HEADS)
        n_t = take(HEADS, KH, STREAMS)
        p_n = take(HEADS, KH)
        bmask = take(STREAMS)
        parity = take(2, P)
        later = take(2, P)
        m_out = take(1 + STREAMS)
        dec_row = take(STREAMS)
        g0 = top[0]
        top[0] = (kh_at := CS * KH * HD)
        fx, lf, b_row, a_row, a2, wu_row, em_row, t_row = (take(T) for _ in range(8))
        top[0] = g0


        top[0] = 0
        x1 = take(KD, T)
        xk = take(KD, T)
        og = xk
        gate = take(KD, T)
        ckv = take(RT, T)
        kpe = take(T)
        cq = take(QT, T)
        rope_c, rope_s = take(T), take(T)
        swap = take(P)
        uv = take(RT, AH * P)
        pe_raw = take(T)
        rot = take(T)
        lsq = take(QT, T)
        kv_tok = take(LAT)
        lrstd, qrstd = take(T), take(T)
        mask_l, mask_r = take16(P), take16(P)
        ones16 = take16(P)
        own_keys = take16(STREAMS, P)
        mask_rows = take(2 * P + STREAMS * P)
        osT = take(RT, AH, STREAMS, STEP)
        q0 = top[0]
        csq = take(QT, T)
        top[0] = q0
        qs = take(3, STREAMS, AH, STEP)
        mx, nmx, rsum, rinv = take(2), take(2), take(2), take(2)
        area[0] = xc[:].rearrange("p a b -> p (a b)")
        top[0] = 0
        xb = take(KD, T)
        top[0] = 0
        pairw = take(17, P)
        uq = pairw[:, 0:9].rearrange("p (a b) c -> p a b c", a=3)
        uk = pairw[:, 9:13].rearrange("p (a b) c -> p a b c", a=2)
        ukt = pairw[:, 13:17].rearrange("p (a b) c -> p a b c", a=2)
        qn = [take(T) for _ in range(2)]
        kn = [take(SEQ) for _ in range(2)]
        vp = take(NP, 2 * P)
        ptm = take(NP, SEQ)
        qz = take(2, T)
        pexp = [take(SEQ) for _ in range(2)]
        top[0] = 0
        keys = [take(10, P) for _ in range(2)]
        qb = [take(3, P) for _ in range(2)]
        pts = [take(3, P) for _ in range(2)]
        pexp_f = [take(3 * P) for _ in range(2)]

        def leave(c, n):
            c.eng.drain().then_inc(stage_left, 1)
            c.eng.wait_ge(stage_left, 5 * n)

        def own_tiles(ap):
            return ap.rearrange("p (b t) -> p b t", t=STEP)

        def x_streams(s, tap, n=STEP):
            return xin[s][:, PROMPT_X:XPW].rearrange("p (b w) -> p b w", w=HIST + STEP)[:, :, tap:tap + n]

        @block.sync
        def _(sp):
            c = Counts(sp)
            for q in range(4):
                op = sp.dma_start(x_a[:, 2 * q:2 * q + 2, :], i["x"][:, 2 * q:2 * q + 2, :])
                op.then_inc(x_in[q], c.up(x_in[q], 16))
            for dst, name in [(vec[:], "vec"), (wq_c[:], "wq"), (wk_c[:], "wk"), (wv_c, "wv"), (gqkv, "gqkv"),
                              (bdmask[:], "bdmask"), (hist, "hist"), (ident[:], "ident")]:
                sp.dma_start(dst, i[name]).then_inc(const_in, c.up(const_in, 16))
            for s in range(SLOTS):
                sp.dma_start(ring[:, s], i["stream"][s]).then_inc(w_in[s], c.up(w_in[s], 16))

            def load_weight(n, s, user):
                if user is not None:
                    sp.wait_ge(user, c.next(user))
                sp.dma_start(ring[:, s], i["stream"][n]).then_inc(w_in[s], c.up(w_in[s], 16))

            def stage_a(j):
                for s in range(SLOTS):
                    load_weight((j + 1) * SLOTS + s, s, A.fill[s % 2])
                for s in range(2):
                    for ready, out, slot, dram in ((vs_ready, v_out, vs, v_dram), (ks_ready, k_out, ks, k_dram),
                                                   (zs_ready, z_out, zs, z_dram)):
                        sp.wait_ge(ready, c.next(ready))
                        src = slot[s] if len(slot[s].shape) == 2 else slot[s].rearrange("p a b -> p (a b)")
                        sp.dma_start(dram[j * 2 + s], src).then_inc(out[s], c.up(out[s], 16))
            c.rounds(NI // 2, stage_a)
            for out in (v_out, k_out, z_out):
                for s in range(2):
                    sp.wait_ge(out[s], c.all(out[s], step=16))
            leave(c, 1)

            for dst, name in ((rowc[0:HEADS], "rows"), (n_t, "n0"), (bmask, "bmask"), (parity, "parity"), (later, "later")):
                sp.dma_start(dst, i[name]).then_inc(misc_in, c.up(misc_in, 16))
            for s in range(CS):
                sp.dma_start(ct[s], i["c0"][s]).then_inc(c_in[s], c.up(c_in[s], 16))
            sp.dma_start(o["conv"], tails[:]).then_inc(out_done, c.up(out_done, 16))
            sp.wait_ge(G.bfree[0], c.next(G.bfree[0]))

            def stage_b(h, last=False):
                op = sp.dma_start(vh.rearrange("p a b c -> p a (b c)"),
                                         v_dram[bass.ts(h, KH)].rearrange("c p n -> p c n"))
                op.then_inc(hv_in, c.up(hv_in, 16))
                op = sp.dma_start(kh.rearrange("p a b c -> p a (b c)"),
                                         k_dram[bass.ts(h, KH)].rearrange("c p n -> p c n"))
                op.then_inc(hk_in, c.up(hk_in, 16))
                if (due := c.all(y_ready)) is not None:
                    sp.wait_ge(y_ready, due)
                sp.dma_start(zh, z_dram[bass.ts(h, KH)].rearrange("c p n -> p c n")).then_inc(hz_in, c.up(hz_in, 16))
                sp.wait_ge(parts_ready, c.next(parts_ready))
                sp.dma_start(vp_dram.rearrange("a p n -> p a n"), v_part).then_inc(parts_out, c.up(parts_out, 16))
                sp.wait_ge(parts_ready, c.next(parts_ready))
                sp.dma_start(kp_dram.rearrange("a p n -> p a n"), k_part).then_inc(parts_out, c.up(parts_out, 16))
                sp.wait_ge(parts_out, c.all(parts_out, step=16))
                for m, (ki, vi) in enumerate(COMBOS):
                    rows = slice(STEP * m, STEP * (m + 1))
                    op = sp.dma_start(k_stack[rows], kp_dram[ki - 1].rearrange("(b t) n -> t b n", t=STEP))
                    op.then_inc(stack_in, c.up(stack_in, 16))
                    op = sp.dma_start(v_stack[rows], vp_dram[vi - 1].rearrange("(b t) n -> t b n", t=STEP))
                    op.then_inc(stack_in, c.up(stack_in, 16))
                c.skip(B.bfree[1], 2)
                for b in range(STREAMS):
                    s = b % CS
                    c.skip(B.bfree[1])
                    sp.wait_ge(B.bfree[1], c.next(B.bfree[1]))
                    sp.dma_start(o["s_c"][h * STREAMS + b], ct[s]).then_inc(c_out[s], c.up(c_out[s], 16))
                    if b + CS < STREAMS or not last:
                        sp.wait_ge(c_out[s], c.all(c_out[s], step=16))
                        sp.dma_start(ct[s], i["c0"][h * STREAMS + (b + CS)]).then_inc(c_in[s], c.up(c_in[s], 16))
                c.skip(B.bfree[0], 19)
                sp.wait_ge(stack_in, c.all(stack_in, step=16))
                for q in range(KH):
                    sp.wait_ge(B.bfree[q % 2], c.next(B.bfree[q % 2]))
                    sp.dma_start(o["p_c"][h * KH + q], cps[q % 2]).then_inc(cp_out[q % 2], c.up(cp_out[q % 2], 16))
                c.skip(y_ready)
            c.rounds(HEADS - 1, stage_b)
            stage_b(HEADS - 1, last=True)
            sp.wait_ge(y_ready, c.all(y_ready))
            for dst, src in ((o["s_n"], n_t), (o["p_n"], p_n), (o["m"], m_out[0:HEADS])):
                sp.dma_start(dst, src).then_inc(out_done, c.up(out_done, 16))
            for s in range(CS):
                sp.wait_ge(c_out[s], c.all(c_out[s], step=16))
            for s in range(2):
                sp.wait_ge(cp_out[s], c.all(cp_out[s], step=16))
            sp.wait_ge(out_done, c.all(out_done, step=16))
            leave(c, 2)

            sp.dma_start(x1, i["x"]).then_inc(x1_in, c.up(x1_in, 16))
            for dst, name in ((rope_c, "cos"), (rope_s, "sin"), (swap, "swap"), (uv, "uv"), (mask_rows[0:1], "masks")):
                sp.dma_start(dst, i[name]).then_inc(late_in, c.up(late_in, 16))

            def stage_c(m):
                for s in range(SLOTS):
                    load_weight((m + 1) * SLOTS + 2 * NI + s, s, C.fill[s // 2] if s % 2 == 0 else None)
            c.rounds(KD // 2, stage_c)
            at = 2 * NI + 2 * KD + SLOTS
            load_weight(at + 0, 0, Dd.fill[0])
            load_weight(at + 1, 1, Dd.fill[1])
            load_weight(at + 2, 2, Dd.fill[0])
            load_weight(at + 3, 3, Dd.fill[1])
            load_weight(at + 4, 0, Dd.fill[0])
            load_weight(at + 5, 1, Dd.fill[1])
            c.rounds(2, lambda m: [load_weight(m * SLOTS + (at + 6 + r), (2 + r) % SLOTS, Dd.fill[r % 2])
                                   for r in range(SLOTS)])
            sp.wait_ge(lat_ready, c.next(lat_ready))
            sp.dma_start(o["ckv"], ckv).then_inc(out_done, c.up(out_done, 16))
            sp.wait_ge(kpe_ready, c.next(kpe_ready))
            sp.dma_start(o["kpe"], kpe[0:ROPE]).then_inc(out_done, c.up(out_done, 16))
            leave(c, 3)

            def stage_e(p):
                if (due := c.all(pair_done)) is not None:
                    sp.wait_ge(pair_done, due)
                sp.dma_start(pairw, i["pairw"][p]).then_inc(pair_in, c.up(pair_in, 16))
                c.skip(pair_done)
            c.rounds(PAIRS, stage_e)
            leave(c, 4)

            def stage_f(m):
                for s in range(2):
                    if (due := c.all(F.fill[s])) is not None:
                        sp.wait_ge(F.fill[s], due)
                    sp.dma_start(keys[s], i["keys"][m * 2 + s]).then_inc(keys_in[s], c.up(keys_in[s], 16))
                    c.skip(F.fill[s])
            c.rounds(STREAMS // 2, stage_f)

            for r in range(SLOTS):
                load_weight(at + 14 + r, (2 + r) % SLOTS, H.fill[r % 2])
            for n in range(KD):
                sp.wait_ge(y_out, c.next(y_out))
                sp.dma_start(o["y"][:, n, :], x1[:, n, :]).then_inc(out_done, c.up(out_done, 16))
            sp.wait_ge(out_done, c.all(out_done, step=16))

        @block.tensor
        def _(pe):
            c = Counts(pe)
            mm = nc.tensor.matmul

            def tokens(buf, lhs, rhs, first, last):
                for a in range(2):
                    done = mm(halves(buf)[:, a, :], lhs, rhs[:, a * HALF:(a + 1) * HALF], start=first, stop=last)
                return done

            def project(bufs, w, slot_k, rhs, n_k, waits=()):
                if (due := c.all(bufs.free[w])) is not None:
                    pe.wait_ge(bufs.free[w], due)
                for k in range(n_k):
                    last = tokens(work[w], slot_k(k), rhs[:, k, :], k == 0, k == n_k - 1)
                last.then_inc(bufs.fill[w], c.up(bufs.fill[w]))
                c.skip(bufs.free[w])

            def sum_squares(bufs, w, sq_tiles, n):
                pe.wait_ge(bufs.free[w], c.all(bufs.free[w]))
                for k in range(n):
                    pe.wait_ge(squares, c.next(squares))
                    last = tokens(work[w], ones_f[:], sq_tiles[:, k, :], k == 0, k == n - 1)
                last.then_inc(bufs.fill[w], c.up(bufs.fill[w]))
                c.skip(bufs.free[w])

            pe.wait_ge(ones_ready, c.next(ones_ready))
            for k in range(KD):
                pe.wait_ge(squares, c.next(squares))
                last = tokens(work[0], ones_f[:], xn[:, k, :], k == 0, k == KD - 1)
            last.then_inc(G.fill[0], c.up(G.fill[0]))
            pe.wait_ge(normed, c.all(normed, ahead=KD))
            pe.wait_ge(basis_ready, c.next(basis_ready))

            def stage_a(j):
                for s in range(2):
                    n = j * 2 + s
                    pe.wait_ge(w_in[2 * s], c.next(w_in[2 * s], step=16))
                    if (due := c.all(A.free[0])) is not None:
                        pe.wait_ge(A.free[0], due)
                    for k in range(KD):
                        last = tokens(work[0], ring[:, 2 * s, k, :], xn[:, k, :], k == 0, k == KD - 1)
                    last.then_inc(A.fill[0], c.up(A.fill[0]))
                    c.skip(A.free[0])
                    pe.wait_ge(w_in[2 * s + 1], c.next(w_in[2 * s + 1], step=16))
                    if (due := c.all(zs_ready)) is not None:
                        pe.wait_ge(zs_ready, due)
                    for k in range(KD):
                        last = tokens(work[1], ring[:, 2 * s + 1, k, :], xn[:, k, :], k == 0, k == KD - 1)
                    last.then_inc(A.fill[1], c.up(A.fill[1]))
                    c.skip(zs_ready)
                    for q, (src, ready) in enumerate(((xin[s], A.free[0]), (xcs[s], xcs_ready))):
                        if q == 0:
                            pe.wait_ge(ready, c.all(ready))
                        else:
                            pe.wait_ge(ready, c.next(ready))
                        if (due := c.all(A.bfree[2 * q])) is not None:
                            pe.wait_ge(A.bfree[2 * q], due)
                        for t in range(TT):
                            if q == 1:
                                lhs = src[:, t * P:(t + 1) * P]
                            elif t < NP:
                                lhs = src[:, HIST + t * P:HIST + (t + 1) * P]
                            else:
                                lhs = xst[s]
                            at = (t % 3) * VG
                            last = mm(bank[2 * q + t // 3][:, at:at + VG], lhs, basis[:, q, n, :], start=True, stop=True)
                        last.then_inc(A.bfill[2 * q], c.up(A.bfill[2 * q]))
                        c.skip(A.bfree[2 * q])
            c.rounds(NI // 2, stage_a)
            leave(c, 1)

            for q in range(2):
                for t in range(TT):
                    last = nc.tensor.transpose(work[q][0:HEADS, t * P:(t + 1) * P],
                                               gacc[:, t, q * HEADS:(q + 1) * HEADS], ident[:])
                last.then_inc(G.fill[q], c.up(G.fill[q]))
            pe.wait_ge(exp_rows, c.next(exp_rows))
            for q, row in enumerate((a_row, em_row, wu_row)):
                for t in range(TT):
                    at = (q * TT + t) * HEADS
                    last = nc.tensor.transpose(bank[0][:, at:at + HEADS], row[0:HEADS, t * P:(t + 1) * P],
                                               ident[0:HEADS, 0:HEADS])
            last.then_inc(G.bfill[0], c.up(G.bfill[0]))
            pe.wait_ge(sel_ready, c.next(sel_ready))
            op = mm(bank[1][:, 0:HEADS * STREAMS], ones_f[0:HEADS, :],
                                decsel[0:HEADS].rearrange("p a b -> p (a b)"), start=True, stop=True)
            op.then_inc(G.bfill[1], c.up(G.bfill[1]))
            pe.wait_ge(G.bfree[0], c.all(G.bfree[0], ahead=1))
            pe.wait_ge(cols_ready, c.all(cols_ready, ahead=1))

            def stage_b(h):
                pe.wait_ge(bd_ready, c.next(bd_ready))
                for q in range(KH):
                    for w, bd in enumerate((bdq, bdk)):
                        if (due := c.all(B.free[w])) is not None:
                            pe.wait_ge(B.free[w], due)
                        last = tokens(work[w], bd[:, q, :], xc[:, h * KH + q, :], True, True)
                        last.then_inc(B.fill[w], c.up(B.fill[w]))
                        c.skip(B.free[w])
                pe.wait_ge(sel_ready, c.next(sel_ready))
                pe.wait_ge(B.free[0], c.all(B.free[0]))
                mm(work[0][:, 0:SEQ], ones_f[0:HEADS, :], msel[0:HEADS, 0:SEQ], start=True, stop=True)
                op = mm(work[0][:, SEQ:T], ones_f[0:HEADS, :], msel[0:HEADS, SEQ:T], start=True, stop=True)
                op.then_inc(B.fill[0], c.up(B.fill[0]))
                c.skip(B.free[0])
                pe.wait_ge(B.free[1], c.all(B.free[1]))
                op = mm(work[1][:, 0:P], ones_f[0:HEADS, :], wisel[0:HEADS, :], start=True, stop=True)
                op.then_inc(B.fill[1], c.up(B.fill[1]))
                c.skip(B.free[1])
                for t in range(TT):
                    b = t % 2
                    if (due := c.all(B.bfree[b])) is not None:
                        pe.wait_ge(B.bfree[b], due)
                    if t == 0:
                        pe.wait_ge(qm_ready, c.next(qm_ready))
                    q0 = t * P
                    for q in range(KH):
                        last = mm(bank[b][:, 0:WID[t]], k_t[:, q, q0:q0 + P], q_t[:, q, q0:q0 + WID[t]],
                                  start=q == 0, stop=q == KH - 1)
                    last.then_inc(B.bfill[b], c.up(B.bfill[b]))
                    c.skip(B.bfree[b])

                def intra(t, out):
                    keys_of = range(t + 1) if t < NP else [NP]
                    for n, s in enumerate(keys_of):
                        lhs = pt[:, OFF[s] + (t - s) * P:OFF[s] + (t - s + 1) * P]
                        end = n == len(keys_of) - 1
                        mm(small[:, S_DEN + t:S_DEN + t + 1], lhs, ones_f[:, 0:1], start=n == 0, stop=end)
                    for n, s in enumerate(keys_of):
                        lhs = pt[:, OFF[s] + (t - s) * P:OFF[s] + (t - s + 1) * P]
                        end = n == len(keys_of) - 1
                        last = mm(out, lhs, vh[:, :, s, :], start=n == 0, stop=end and t < NP,
                                  skip_group_check=t == NP)
                    return last

                pe.wait_ge(B.bfree[0], c.all(B.bfree[0]))
                pe.wait_ge(B.bfree[1], c.all(B.bfree[1]))
                pe.wait_ge(B.free[1], c.all(B.free[1]))
                pe.wait_ge(hv_in, c.next(hv_in, step=16))
                if (due := c.all(B.bfree[3])) is not None:
                    pe.wait_ge(B.bfree[3], due)
                intra(NP, bank[3][:, :])
                for q in range(KH):
                    for par in range(2):
                        mm(small[:, S_NQ:S_NQ + STREAMS], qm[:, q, par, :], n_t[:, h, q, :],
                           start=q == 0 and par == 0, stop=q == KH - 1 and par == 1)

                def prompt_tile(t):
                    if (due := c.all(B.bfree[2])) is not None:
                        pe.wait_ge(B.bfree[2], due)
                    intra(t, bank[2][:, :]).then_inc(B.bfill[2], c.up(B.bfill[2]))
                    c.skip(B.bfree[2])

                def turn(t):
                    pe.wait_ge(B.bfree[2] if t < NP else B.bfree[3], c.all(B.bfree[2] if t < NP else B.bfree[3]))
                    pe.wait_ge(B.free[0], c.all(B.free[0]))
                    for q in range(KH):
                        last = nc.tensor.transpose(work[0][:, q * P:(q + 1) * P], hn[:, q * P:(q + 1) * P], ident[:])
                    last.then_inc(B.fill[0], c.up(B.fill[0]))
                    c.skip(B.free[0])

                def stream(b):
                    s, g = b % CS, 32 * (b // 2)
                    pe.wait_ge(c_in[s], c.next(c_in[s], step=16))
                    for q in range(KH):
                        last = mm(bank[3][g:g + 32, :], qm[:, q, b % 2, g:g + 32], ct[s][:, q, :], start=False,
                                  stop=b == STREAMS - 1 and q == KH - 1, skip_group_check=True, tile_position=(0, g))
                    if b == STREAMS - 1:
                        last.then_inc(B.bfill[3], c.up(B.bfill[3]))
                        c.skip(B.bfree[3])
                    if b == 0:
                        pe.wait_ge(stack_in, c.all(stack_in, ahead=2 * len(COMBOS), step=16))
                        c.skip(stack_in, 2 * len(COMBOS), 16)
                    for q in range(KH):
                        pe.wait_ge(B.bfree[q % 2], c.all(B.bfree[q % 2]))
                        mm(bank[q % 2][:, :], k_stack[:, b, q * P:(q + 1) * P], v_stack[:, b, :],
                                                start=True, stop=True).then_inc(B.bfill[q % 2], c.up(B.bfill[q % 2]))
                        c.skip(B.bfree[q % 2])

                def new_n():
                    pe.wait_ge(kwsum_ready, c.next(kwsum_ready))
                    pe.wait_ge(kw_ready, c.next(kw_ready))
                    pe.wait_ge(kw_ready, c.next(kw_ready))
                    for q in range(KH):
                        at = S_NS + q * STREAMS
                        mm(small[:, at:at + STREAMS], kh[:, q, NP, :], bmask, start=True, stop=True)
                        mm(small[:, S_NP + q:S_NP + q + 1], kwsum[:, q, :], ones_f[:, 0:1], start=True, stop=True)

                def prompt_c(q):
                    pe.wait_ge(B.bfree[q % 2], c.all(B.bfree[q % 2]))
                    for t in range(NP):
                        last = mm(bank[q % 2][:, :], kh[:, q, t, :], vh[:, :, t, :], start=t == 0, stop=t == NP - 1)
                    last.then_inc(B.bfill[q % 2], c.up(B.bfill[q % 2]))
                    c.skip(B.bfree[q % 2])

                prompt_tile(0)
                stream(0)
                stream(1)
                turn(0)
                prompt_tile(1)
                stream(2)
                turn(1)
                prompt_tile(2)
                stream(3)
                turn(2)
                prompt_tile(3)
                stream(4)
                turn(3)
                new_n()
                stream(5)
                stream(6)
                stream(7)
                for q in range(KH):
                    prompt_c(q)
                turn(NP)
                c.skip(B.free[1])
            c.rounds(HEADS, stage_b)
            leave(c, 2)

            def stage_c(m):
                for s in range(2):
                    if (due := c.all(C.free[s])) is not None:
                        pe.wait_ge(C.free[s], due)
                    for q in range(NI):
                        if q % KD == 0:
                            pe.wait_ge(w_in[2 * s + q // KD], c.next(w_in[2 * s + q // KD], step=16))
                        last = tokens(work[s], ring[:, 2 * s + q // KD, q % KD, :], xc[:, q, :], q == 0, q == NI - 1)
                    last.then_inc(C.fill[s], c.up(C.fill[s]))
                    c.skip(C.free[s])
            c.rounds(KD // 2, stage_c)

            pe.wait_ge(C.free[0], c.all(C.free[0]))
            for k in range(KD):
                pe.wait_ge(squares, c.next(squares))
                last = tokens(work[0], ones_f[:], gate[:, k, :], k == 0, k == KD - 1)
            last.then_inc(G.bfill[2], c.up(G.bfill[2]))
            pe.wait_ge(normed, c.all(normed, ahead=2 * KD))
            c.skip(root, 2)

            def weights(slot):
                pe.wait_ge(w_in[slot], c.next(w_in[slot], step=16))
                return lambda k: ring[:, slot, k, :]

            project(Dd, 0, weights(0), xk, KD)
            project(Dd, 1, weights(1), xk, KD)
            project(Dd, 0, weights(2), xk, KD)
            pe.wait_ge(normed, c.all(normed, ahead=3 * KD))
            project(Dd, 1, weights(3), xb, KD)
            project(Dd, 0, weights(0), xb, KD)
            project(Dd, 1, weights(1), xb, KD)
            pe.wait_ge(Dd.free[0], c.all(Dd.free[0]))
            for k in range(RT):
                pe.wait_ge(squares, c.next(squares))
                last = tokens(work[0], ones_f[:], lsq[:, k, :], k == 0, k == RT - 1)
            last.then_inc(G.bfill[3], c.up(G.bfill[3]))
            pe.wait_ge(Dd.free[1], c.all(Dd.free[1]))
            tokens(work[1], swap, pe_raw, True, True).then_inc(rope_mm, c.up(rope_mm))
            pe.wait_ge(root, c.next(root))
            for k in range(QT):
                pe.wait_ge(squares, c.next(squares))
                last = tokens(work[0], ones_f[:], csq[:, k, :], k == 0, k == QT - 1)
            last.then_inc(G.bfill[3], c.up(G.bfill[3]))
            pe.wait_ge(root, c.next(root))
            pe.wait_ge(kpe_ready, c.next(kpe_ready))

            def stage_d(m):
                for r in range(SLOTS):
                    project(Dd, r % 2, weights((2 + r) % SLOTS), xb, KD)
            c.rounds(2, stage_d)
            pe.wait_ge(lat_ready, c.next(lat_ready))
            for r in range(RT):
                last = nc.tensor.transpose(bank[0][:, r * P:(r + 1) * P], ckv[:, r, SEQ:T], ident[:])
            last.then_inc(Dd.bfill[0], c.up(Dd.bfill[0]))
            leave(c, 3)

            def stage_e(p):
                pe.wait_ge(pair_in, c.next(pair_in, step=16))
                project(E, 0, lambda k: uq[:, 0, k, :], cq, QT)
                project(E, 1, lambda k: uq[:, 1, k, :], cq, QT)
                project(E, 0, lambda k: uq[:, 2, k, :], cq, QT)
                for a in range(2):
                    w = 1 - a
                    pe.wait_ge(E.free[w], c.all(E.free[w]))
                    for r in range(RT):
                        last = mm(work[w][:, 0:SEQ], uk[:, a, r, :], ckv[:, r, 0:SEQ], start=r == 0, stop=r == RT - 1)
                    last.then_inc(E.fill[w], c.up(E.fill[w]))
                    c.skip(E.free[w])
                pe.wait_ge(E.free[0], c.all(E.free[0]))
                pe.wait_ge(E.free[1], c.all(E.free[1]))
                tokens(work[1], swap, pe_raw, True, True).then_inc(E.fill[1], c.up(E.fill[1]))
                c.skip(E.free[1])
                pe.wait_ge(E.free[0], c.all(E.free[0]))
                for t in range(NP):
                    for r in range(RT):
                        last = mm(work[0][:, t * 2 * P:(t + 1) * 2 * P], ckv[:, r, t * P:(t + 1) * P],
                                  uv[:, r, bass.ts(p, 2 * P)], start=r == 0, stop=r == RT - 1)
                last.then_inc(E.fill[0], c.up(E.fill[0]))
                c.skip(E.free[0])
                pe.wait_ge(E.free[1], c.all(E.free[1]))
                for a in range(2):
                    for r in range(RT):
                        at = (2 * a + r) * P
                        last = mm(work[1][:, at:at + P], ukt[:, a, r, :], qn[a][:, SEQ:T], start=True, stop=True)
                last.then_inc(E.fill[1], c.up(E.fill[1]))
                c.skip(E.free[1])

                def scores(u):
                    a, t = divmod(u, NP)
                    n = (t + 1) * P
                    b = u % 2
                    if u == 0:
                        pe.wait_ge(qz_ready, c.next(qz_ready))
                    if (due := c.all(E.bfree[b])) is not None:
                        pe.wait_ge(E.bfree[b], due)
                    mm(bank[b][:, 0:n], qn[a][:, t * P:(t + 1) * P], kn[a][:, 0:n], start=True, stop=False)
                    mm(bank[b][:, n - P:n], mask_l[0:1, :], mask_r[0:1, :], start=False, stop=False)
                    op = mm(bank[b][:, 0:n], qz[:, a, t * P:(t + 1) * P], kpe[:, 0:n], start=False, stop=True)
                    op.then_inc(E.bfill[b], c.up(E.bfill[b]))
                    c.skip(E.bfree[b])

                def turn(u):
                    t, b = u % NP, 2 + u % 2
                    pe.wait_ge(prob_ready, c.next(prob_ready))
                    if (due := c.all(E.bfree[b])) is not None:
                        pe.wait_ge(E.bfree[b], due)
                    for s in range(t + 1):
                        last = nc.tensor.transpose(bank[b][:, s * P:(s + 1) * P], pexp[u % 2][:, s * P:(s + 1) * P], ident[:])
                    last.then_inc(E.bfill[b], c.up(E.bfill[b]))
                    c.skip(E.bfree[b])

                def outputs(a):
                    pe.wait_ge(E.bfree[2], c.all(E.bfree[2]))
                    pe.wait_ge(E.bfree[3], c.all(E.bfree[3]))
                    pe.wait_ge(E.free[a], c.all(E.free[a]))
                    for s in range(NP):
                        last = mm(work[a][:, s * P:SEQ], vp[:, s, a * P:(a + 1) * P], ptm[:, s, s * P:SEQ],
                                  start=s == 0, stop=True, skip_group_check=True)
                    last.then_inc(E.fill[a], c.up(E.fill[a]))
                    c.skip(E.free[a])

                scores(0)
                for u in range(1, 2 * NP):
                    scores(u)
                    turn(u - 1)
                    if u == NP:
                        outputs(0)
                turn(2 * NP - 1)
                outputs(1)
            c.rounds(PAIRS, stage_e)
            leave(c, 4)

            def stage_f(m):
                for s in range(2):
                    b = m * 2 + s
                    pe.wait_ge(keys_in[s], c.next(keys_in[s], step=16))
                    pe.wait_ge(qb_ready, c.next(qb_ready))
                    if (due := c.all(F.bfree[s])) is not None:
                        pe.wait_ge(F.bfree[s], due)
                    for r in range(RT):
                        mm(bank[s][:, 0:PAST], qb[s][:, r, :], keys[s][:, 2 * r:2 * r + 2, :], start=r == 0, stop=False)
                    mm(bank[s][:, 0:PAST], qb[s][:, 2, :], keys[s][:, 4:6, :], start=False, stop=True)
                    for r in range(RT):
                        mm(bank[s][:, PAST:PAST + P], qb[s][:, r, :], ckv[:, r, SEQ:T], start=r == 0, stop=False)
                    mm(bank[s][:, PAST:PAST + P], qb[s][:, 2, :], kpe[:, SEQ:T], start=False, stop=False)
                    mm(bank[s][:, PAST:PAST + P], ones16[0:1, :], own_keys[0:1, b, :],
                                        start=False, stop=True).then_inc(F.bfill[s], c.up(F.bfill[s]))
                    c.skip(F.bfree[s])
                for s in range(2):
                    pe.wait_ge(prob_ready, c.next(prob_ready))
                    if (due := c.all(F.bfree[2 + s])) is not None:
                        pe.wait_ge(F.bfree[2 + s], due)
                    for q in range(3):
                        last = nc.tensor.transpose(bank[2 + s][:, q * P:(q + 1) * P], pexp_f[s][:, q * P:(q + 1) * P], ident[:])
                    last.then_inc(F.bfill[2 + s], c.up(F.bfill[2 + s]))
                    c.skip(F.bfree[2 + s])
                for s in range(2):
                    pe.wait_ge(F.bfree[2 + s], c.all(F.bfree[2 + s]))
                    if (due := c.all(F.free[s])) is not None:
                        pe.wait_ge(F.free[s], due)
                    for r in range(RT):
                        for q in range(3):
                            lhs = keys[s][:, 6 + 2 * q + r, :] if q < 2 else kv_tok[:, r * P:(r + 1) * P]
                            last = mm(work[s][:, r * P:(r + 1) * P], lhs, pts[s][:, q, :], start=q == 0, stop=q == 2)
                    last.then_inc(F.fill[s], c.up(F.fill[s]))
                    c.skip(F.free[s])
            c.rounds(STREAMS // 2, stage_f)
            for s in range(2):
                pe.wait_ge(F.free[s], c.all(F.free[s]))
                pe.wait_ge(F.bfree[s], c.all(F.bfree[s]))
            for h in range(AH):
                for r in range(RT):
                    at = (h % 4) * P
                    last = mm(bank[h // 4][:, at:at + P], uv[:, r, h * P:(h + 1) * P],
                              osT[:, r, h].rearrange("p b t -> p (b t)"), start=r == 0, stop=r == RT - 1)
                if h % 4 == 3:
                    last.then_inc(H.bfill[h // 4], c.up(H.bfill[h // 4]))
            pe.wait_ge(H.bfree[0], c.all(H.bfree[0], ahead=1))
            pe.wait_ge(H.bfree[1], c.all(H.bfree[1], ahead=1))

            c.rounds(2, lambda m: [project(H, r % 2, weights((2 + r) % SLOTS), og, KD) for r in range(SLOTS)])
            pe.wait_ge(H.free[0], c.all(H.free[0]))
            for k in range(KD):
                pe.wait_ge(squares, c.next(squares))
                last = tokens(work[0], ones_f[:], gate[:, k, :], k == 0, k == KD - 1)
            last.then_inc(H.bfill[2], c.up(H.bfill[2]))

        @block.scalar
        def _(act):
            c = Counts(act)

            def inverse_rms(buf, width):
                op = nc.scalar.activation(two(rstd[:]), halves(buf), ACT.Sqrt, bias=eps_t[:], scale=1.0 / width)
                op.then_inc(root, c.up(root))

            for k in range(KD):
                act.wait_ge(x_in[k // 2], c.all(x_in[k // 2], ahead=1, step=16))
                nc.scalar.activation(xn[:, k, :], x_a[:, k, :], ACT.Square).then_inc(squares, c.up(squares))
            act.wait_ge(ones_ready, c.next(ones_ready))
            act.wait_ge(G.fill[0], c.next(G.fill[0]))
            inverse_rms(work[0], D)
            act.wait_ge(const_in, c.all(const_in, ahead=8, step=16))

            def stage_a(j):
                for s in range(2):
                    n = j * 2 + s
                    if (due := c.all(A.bfill[0], ahead=-1)) is not None:
                        act.wait_ge(A.bfill[0], due)
                    if (due := c.all(tail_kept, ahead=-1)) is not None:
                        act.wait_ge(tail_kept, due)
                    act.wait_ge(A.fill[0], c.next(A.fill[0]))
                    nc.scalar.activation(x_streams(s, 0, HIST), hist[:, n], ACT.Copy).then_inc(act_own, c.up(act_own))
                    op = nc.scalar.activation(xin[s][:, HIST:HIST + HALF], halves(work[0])[:, 0, :], ACT.Copy)
                    op.then_inc(act_own, c.up(act_own))
                    op = nc.scalar.activation(xin[s][:, HIST + HALF:PROMPT_X],
                                              halves(work[0])[:, 1, 0:SEQ - HALF], ACT.Copy)
                    op.then_inc(act_own, c.up(act_own))
                    op = nc.scalar.activation(xst[s], halves(work[0])[:, 1, SEQ - HALF:HALF], ACT.Copy)
                    op.then_inc(act_own, c.up(act_own))
                    op = nc.scalar.activation(x_streams(s, HIST),
                                              own_tiles(halves(work[0])[:, 1, SEQ - HALF:HALF]), ACT.Copy)
                    op.then_inc(A.free[0], c.up(A.free[0]))
                    act.wait_ge(act_own, c.all(act_own))
                    act.wait_ge(A.free[0], c.all(A.free[0]))
                    w0 = vec[:, bass.ds(n * TAPS + V_CONV, 1)]
                    b0 = vec[:, bass.ds(n + V_CB, 1)]
                    op = nc.scalar.activation(acc[s][:, 0:SEQ], xin[s][:, 0:SEQ], ACT.Identity, scale=w0, bias=b0)
                    op.then_inc(act_own, c.up(act_own))
                    op = nc.scalar.activation(own_tiles(acc[s][:, SEQ:T]), x_streams(s, 0), ACT.Identity,
                                              scale=w0, bias=b0)
                    op.then_inc(tap0, c.up(tap0))
                    if (due := c.all(A.bfill[2], ahead=-1)) is not None:
                        act.wait_ge(A.bfill[2], due)
                    if (due := c.all(xc_kept, ahead=-1)) is not None:
                        act.wait_ge(xc_kept, due)
                    act.wait_ge(conv_done, c.next(conv_done))
                    nc.scalar.activation(xcs[s], acc[s], ACT.Silu).then_inc(xcs_ready, c.up(xcs_ready))
                    act.wait_ge(A.fill[1], c.next(A.fill[1]))
                    if (due := c.all(z_out[s], step=16)) is not None:
                        act.wait_ge(z_out[s], due)
                    nc.scalar.activation(two(zs[s]), halves(work[1]), ACT.Silu).then_inc(zs_ready, c.up(zs_ready))
                    c.skip(z_out[s], step=16)
                    for q in (A.bfill[0], A.bfill[2], tail_kept, xc_kept):
                        c.skip(q)
            c.rounds(NI // 2, stage_a)
            leave(c, 1)

            R = slice(0, HEADS)
            act.wait_ge(misc_in, c.next(misc_in, step=16))
            act.wait_ge(misc_in, c.all(misc_in, ahead=4, step=16))
            act.wait_ge(G.fill[1], c.next(G.fill[1]))
            op = nc.scalar.activation(fx[R], work[1][R, 0:T], ACT.Identity, bias=rowc[R, R_BF:R_BF + 1])
            op.then_inc(act_own, c.up(act_own))
            act.wait_ge(act_own, c.all(act_own))
            nc.scalar.activation(t_row[R], fx[R], ACT.Abs).then_inc(act_own, c.up(act_own))
            act.wait_ge(act_own, c.all(act_own))
            nc.scalar.activation(t_row[R], t_row[R], ACT.Exp, scale=-1.0).then_inc(act_own, c.up(act_own))
            act.wait_ge(act_own, c.all(act_own))
            nc.scalar.activation(t_row[R], t_row[R], ACT.Ln, bias=ones_f[R, 0:1]).then_inc(softplus, c.up(softplus))
            act.wait_ge(exp_args, c.next(exp_args))
            nc.scalar.activation(wu_row[R], wu_row[R], ACT.Exp).then_inc(act_own, c.up(act_own))
            nc.scalar.activation(em_row[R], em_row[R], ACT.Exp, scale=-1.0).then_inc(act_own, c.up(act_own))
            nc.scalar.activation(wi_row[R], wi_row[R], ACT.Exp).then_inc(act_own, c.up(act_own))
            nc.scalar.activation(dec_row[R], dec_row[R], ACT.Exp).then_inc(exp_rows, c.up(exp_rows))
            act.wait_ge(G.bfree[0], c.all(G.bfree[0], ahead=1))

            def stage_b(h):
                def weigh_k(t, done=act_own):
                    op = nc.scalar.activation(kh[:, :, t, :], kh[:, :, t, :], ACT.Copy,
                                              scale=cols[:, 2, t, bass.ds(h, 1)])
                    op.then_inc(done, c.up(done))

                for q in range(KH):
                    act.wait_ge(B.fill[0], c.next(B.fill[0]))
                    op = nc.scalar.activation(two(q_t[:, q, :]), halves(work[0]), ACT.Copy)
                    op.then_inc(B.free[0], c.up(B.free[0]))
                    if q == 1:
                        act.wait_ge(hk_in, c.next(hk_in, step=16))
                        weigh_k(NP, kw_ready)
                for t in range(NP):
                    weigh_k(t, kw_ready if t == NP - 1 else act_own)
                act.wait_ge(B.fill[0], c.next(B.fill[0]))
                act.wait_ge(dmax_ready, c.next(dmax_ready))
                for t in range(TT):
                    a_s = cols[:, 0, t, bass.ds(h, 1)]
                    own = pt[:, OFF[t]:OFF[t] + P]
                    nc.scalar.activation(own, own, ACT.Exp, bias=a_s, scale=-1.0).then_inc(act_own, c.up(act_own))
                for t in range(NP - 1):
                    a_s = cols[:, 0, t, bass.ds(h, 1)]
                    raised = B.free[0] if t == NP - 2 else act_own
                    op = nc.scalar.activation(pt[:, OFF[t] + P:OFF[t] + WID[t]], work[0][:, (t + 1) * P:SEQ],
                                              ACT.Exp, bias=a_s, scale=-1.0)
                    op.then_inc(raised, c.up(raised))

                def turned(t):
                    act.wait_ge(B.fill[0], c.next(B.fill[0]))
                    for q in range(KH):
                        raised = B.free[0] if q == KH - 1 else act_own
                        op = nc.scalar.activation(h_t[:, q, t * P:(t + 1) * P],
                                                  work[0][:, q * P:(q + 1) * P], ACT.Copy, scale=head_on[:, q:q + 1])
                        op.then_inc(raised, c.up(raised))

                op = nc.scalar.activation(head_on, vec[:, bass.ds(h * KH + V_ON, KH)], ACT.Copy)
                op.then_inc(act_own, c.up(act_own))
                act.wait_ge(act_own, c.all(act_own))
                if (due := c.all(y_ready)) is not None:
                    act.wait_ge(y_ready, due)
                for t in range(NP):
                    turned(t)
                for q in range(KH):
                    c.skip(B.bfill[q % 2], (19, 18)[q % 2] if q < 2 else 0)
                    act.wait_ge(B.bfill[q % 2], c.next(B.bfill[q % 2]))
                    if (due := c.all(cp_out[q % 2], step=16)) is not None:
                        act.wait_ge(cp_out[q % 2], due)
                    op = nc.scalar.activation(cps[q % 2], bank[q % 2][:, :], ACT.Copy)
                    op.then_inc(B.bfree[q % 2], c.up(B.bfree[q % 2]))
                    c.skip(cp_out[q % 2], step=16)
                turned(NP)
                c.skip(y_ready)
            c.rounds(HEADS, stage_b)
            leave(c, 2)

            def stage_c(m):
                for s in range(2):
                    act.wait_ge(C.free[s], c.next(C.free[s]))
                    op = nc.scalar.activation(gate[:, m * 2 + s, :], x1[:, m * 2 + s, :], ACT.Square)
                    op.then_inc(squares, c.up(squares))
            c.rounds(KD // 2, stage_c)

            act.wait_ge(G.bfill[2], c.next(G.bfill[2]))
            inverse_rms(work[0], D)
            for n in range(RT + 1 + QT):
                w = n % 2
                dst = ckv[:, n, :] if n < RT else pe_raw if n == RT else cq[:, n - RT - 1, :]
                act.wait_ge(Dd.fill[w], c.next(Dd.fill[w]))
                nc.scalar.activation(two(dst), halves(work[w]), ACT.Copy).then_inc(Dd.free[w], c.up(Dd.free[w]))
                if n != RT:
                    act.wait_ge(Dd.free[w], c.all(Dd.free[w]))
                    op = nc.scalar.activation(lsq[:, n, :] if n < RT else csq[:, n - RT - 1, :], dst, ACT.Square)
                    op.then_inc(squares, c.up(squares))
            for m, (out, width) in enumerate(((lrstd, LAT), (qrstd, QLORA))):
                act.wait_ge(G.bfill[3], c.next(G.bfill[3]))
                op = nc.scalar.activation(two(out), halves(work[0]), ACT.Sqrt, bias=eps_t[:], scale=1.0 / width)
                op.then_inc(root, c.up(root))

            def stage_d(m):
                for r in range(SLOTS):
                    act.wait_ge(Dd.fill[r % 2], c.next(Dd.fill[r % 2]))
                    op = nc.scalar.activation(two(gate[:, m * SLOTS + r, :]), halves(work[r % 2]), ACT.Silu)
                    op.then_inc(Dd.free[r % 2], c.up(Dd.free[r % 2]))
            c.rounds(2, stage_d)
            act.wait_ge(Dd.bfill[0], c.next(Dd.bfill[0]))
            nc.scalar.activation(kv_tok, bank[0][:, 0:LAT], ACT.Copy).then_inc(act_own, c.up(act_own))
            leave(c, 3)

            def exponentials(bufs, b, out, n):
                act.wait_ge(max_ready, c.next(max_ready))
                op = nc.scalar.activation(out, bank[b][:, 0:n], ACT.Exp, bias=nmx[:, b:b + 1], scale=ASCALE,
                                          accum_out=rsum[:, b:b + 1])
                op.then_inc(bufs.bfree[b], c.up(bufs.bfree[b]))

            def stage_e(p):
                for w, dst in ((0, qn[0]), (1, qn[1]), (0, pe_raw)):
                    act.wait_ge(E.fill[w], c.next(E.fill[w]))
                    nc.scalar.activation(two(dst), halves(work[w]), ACT.Copy).then_inc(E.free[w], c.up(E.free[w]))
                act.wait_ge(E.fill[0], c.next(E.fill[0]))
                act.wait_ge(E.fill[0], c.next(E.fill[0]))
                op = nc.scalar.activation(vp.rearrange("p a b -> p (a b)"), work[0][:, :], ACT.Copy)
                op.then_inc(E.free[0], c.up(E.free[0]))

                def turned(u):
                    t, b = u % NP, 2 + u % 2
                    act.wait_ge(E.bfill[b], c.next(E.bfill[b]))
                    op = nc.scalar.activation(ptm[:, 0:t + 1, t * P:(t + 1) * P],
                                              bank[b][:, 0:(t + 1) * P].rearrange("p (a b) -> p a b", b=P), ACT.Copy)
                    op.then_inc(E.bfree[b], c.up(E.bfree[b]))

                for u in range(2 * NP):
                    exponentials(E, u % 2, pexp[u % 2][:, 0:(u % NP + 1) * P], (u % NP + 1) * P)
                    if u:
                        turned(u - 1)
                turned(2 * NP - 1)
                c.skip(E.fill[0])
                c.skip(E.fill[1], 4)
            c.rounds(PAIRS, stage_e)
            leave(c, 4)

            def stage_f(m):
                for s in range(2):
                    op = nc.scalar.activation(qb[s], qs[:, :, m * 2 + s].rearrange("p a h t -> p a (h t)"), ACT.Copy)
                    op.then_inc(qb_ready, c.up(qb_ready))
                for s in range(2):
                    exponentials(F, s, pexp_f[s], 3 * P)
                for s in range(2):
                    if (due := c.all(F.fill[s])) is not None:
                        act.wait_ge(F.fill[s], due)
                    act.wait_ge(F.bfill[2 + s], c.next(F.bfill[2 + s]))
                    op = nc.scalar.activation(pts[s].rearrange("p a b -> p (a b)"), bank[2 + s][:, 0:3 * P], ACT.Copy)
                    op.then_inc(F.bfree[2 + s], c.up(F.bfree[2 + s]))
                    c.skip(F.fill[s])
            c.rounds(STREAMS // 2, stage_f)

            def stage_h(m):
                for r in range(SLOTS):
                    act.wait_ge(H.free[r % 2], c.next(H.free[r % 2]))
                    op = nc.scalar.activation(gate[:, m * SLOTS + r, :], x1[:, m * SLOTS + r, :], ACT.Square)
                    op.then_inc(squares, c.up(squares))
            c.rounds(2, stage_h)
            act.wait_ge(H.bfill[2], c.next(H.bfill[2]))
            inverse_rms(work[0], D)

        @block.vector
        def _(dve):
            c = Counts(dve)
            v = nc.vector

            def invert(out):
                dve.wait_ge(root, c.next(root))
                v.reciprocal(out, out).then_inc(dve_own, c.up(dve_own))
                dve.wait_ge(dve_own, c.all(dve_own))

            def scale_norm(out, src, w_col, inv, k, done):
                v.scalar_tensor_tensor(out[:, k, :], src[:, k, :], vec[:, w_col + k:w_col + k + 1], inv,
                                                  ALU.mult, ALU.mult).then_inc(done, c.up(done))

            v.memset(gacc[:], 0.0).then_inc(dve_own, c.up(dve_own))
            dve.wait_ge(const_in, c.all(const_in, ahead=8, step=16))
            for s in range(2):
                v.memset(xin[s][:, 0:HIST], 0.0).then_inc(dve_own, c.up(dve_own))
            invert(rstd[:])
            for k in range(KD):
                scale_norm(xn, x_a, V_AN, rstd[:], k, normed)
            for q, w in enumerate((wq_c[:, 0:NI], wk_c[:, 0:NI], wv_c)):
                op = v.tensor_tensor(gprod[:, q], gqkv[:, q], w.unsqueeze(3).to_broadcast([P, NI, 4, G8]), ALU.mult)
                op.then_inc(dve_own, c.up(dve_own))
            dve.wait_ge(dve_own, c.all(dve_own))
            for q in range(3):
                op = v.tensor_tensor(gprod[:, q, :, 0:2], gprod[:, q, :, 0:2], gprod[:, q, :, 2:4], ALU.add)
                op.then_inc(dve_own, c.up(dve_own))
            dve.wait_ge(dve_own, c.all(dve_own))
            for q in range(2):
                op = v.tensor_tensor(gprod[:, q, :, 0], gprod[:, q, :, 0], gprod[:, q, :, 1], ALU.add)
                op.then_inc(dve_own, c.up(dve_own))
            op = v.tensor_tensor(basis[:, 0, :, P:VG], gprod[:, 2, :, 0], gprod[:, 2, :, 1], ALU.add)
            op.then_inc(dve_own, c.up(dve_own))
            v.tensor_scalar(wk_c[:], wk_c[:], KSCALE, None, ALU.mult).then_inc(dve_own, c.up(dve_own))
            dve.wait_ge(dve_own, c.all(dve_own))
            op = v.tensor_tensor(basis[:, 1, :, P:VG], gprod[:, 0, :, 0], gprod[:, 1, :, 0], ALU.add)
            op.then_inc(dve_own, c.up(dve_own))
            for q, w in enumerate((wv_c, wk_c[:, 0:NI])):
                for n in range(NI):
                    last = v.tensor_tensor(basis[:, q, n, 0:P].rearrange("p (a b) -> p a b", b=4), bdmask[:],
                                           w[:, n].unsqueeze(1).to_broadcast([P, 32, 4]), ALU.mult)
                    raised = basis_ready if q == 1 and n == NI - 1 else dve_own
                    last.then_inc(raised, c.up(raised))

            def stage_a(j):
                for s in range(2):
                    n = j * 2 + s
                    dve.wait_ge(tap0, c.next(tap0))
                    for tap in range(1, TAPS):
                        w = vec[:, bass.ds(n * TAPS + (V_CONV + tap), 1)]
                        a0, a1 = acc[s][:, 0:SEQ], own_tiles(acc[s][:, SEQ:T])
                        op = v.scalar_tensor_tensor(a0, xin[s][:, tap:tap + SEQ], w, a0, ALU.mult, ALU.add)
                        op.then_inc(dve_own, c.up(dve_own))
                        raised = conv_done if tap == TAPS - 1 else dve_own
                        op = v.scalar_tensor_tensor(a1, x_streams(s, tap), w, a1, ALU.mult, ALU.add)
                        op.then_inc(raised, c.up(raised))
                        if tap < TAPS - 1:
                            dve.wait_ge(dve_own, c.all(dve_own))
                    for q, (slot, ready, out) in enumerate(((vs, vs_ready, v_out), (ks, ks_ready, k_out))):
                        dve.wait_ge(A.bfill[2 * q], c.next(A.bfill[2 * q]))
                        if (due := c.all(out[s], step=16)) is not None:
                            dve.wait_ge(out[s], due)
                        c.skip(out[s], step=16)
                        parts = [(slice(0, 3), bank[2 * q][:, 0:3 * VG]), (slice(3, TT), bank[2 * q + 1][:, 0:2 * VG])]
                        parts = [(t, b.rearrange("p (a b) -> p a b", b=VG)) for t, b in parts]
                        for m, (t, b) in enumerate(parts):
                            raised = ready if m else dve_own
                            v.tensor_copy(slot[s][:, t, :], b[:, :, 0:P]).then_inc(raised, c.up(raised))
                        dve.wait_ge(dve_own, c.all(dve_own))
                        if (due := c.all(A.bfree[0])) is not None:
                            dve.wait_ge(A.bfree[0], due)
                        if (due := c.all(A.bfree[2])) is not None:
                            dve.wait_ge(A.bfree[2], due)
                        for m, (t, b) in enumerate(parts):
                            raised = A.bfree[2 * q] if m else dve_own
                            op = v.tensor_tensor(gacc[:, t, :], gacc[:, t, :], b[:, :, P:VG], ALU.add)
                            op.then_inc(raised, c.up(raised))
            c.rounds(NI // 2, stage_a)
            leave(c, 1)

            R = slice(0, HEADS)
            keep, reset = rowc[R, R_KEEP:R_KEEP + T], rowc[R, R_RESET:R_RESET + T]
            m0 = rowc[R, R_M0 + 1:R_M0 + 1 + STREAMS]

            def frames(row):
                return own_tiles(row[R, SEQ:T])

            dve.wait_ge(misc_in, c.next(misc_in, step=16))
            dve.wait_ge(misc_in, c.all(misc_in, ahead=4, step=16))
            v.memset(half_neg, -0.5).then_inc(dve_own, c.up(dve_own))
            dve.wait_ge(G.fill[0], c.next(G.fill[0]))
            dve.wait_ge(G.fill[0], c.next(G.fill[0]))
            op = v.tensor_scalar(a_row[R], work[0][R, 0:T], rowc[R, R_BI:R_BI + 1], None, ALU.add)
            op.then_inc(dve_own, c.up(dve_own))
            dve.wait_ge(softplus, c.next(softplus))
            op = v.scalar_tensor_tensor(lf[R], fx[R], 0.0, t_row[R], ALU.min, ALU.subtract)
            op.then_inc(dve_own, c.up(dve_own))
            dve.wait_ge(dve_own, c.all(dve_own))
            v.tensor_tensor_scan(b_row[R], keep, lf[R], 0.0, ALU.mult, ALU.add).then_inc(dve_own, c.up(dve_own))
            dve.wait_ge(dve_own, c.all(dve_own))
            v.tensor_tensor(a_row[R], a_row[R], b_row[R], ALU.subtract).then_inc(dve_own, c.up(dve_own))
            dve.wait_ge(dve_own, c.all(dve_own))
            v.tensor_copy(a2[R], a_row[R]).then_inc(dve_own, c.up(dve_own))
            dve.wait_ge(dve_own, c.all(dve_own))
            v.tensor_scalar(a2[R, 0:1], a_row[R, 0:1], 0.0, None, ALU.max).then_inc(dve_own, c.up(dve_own))
            v.tensor_tensor(frames(a2)[:, :, 0], frames(a_row)[:, :, 0], m0, ALU.max).then_inc(dve_own, c.up(dve_own))
            dve.wait_ge(dve_own, c.all(dve_own))
            v.tensor_tensor_scan(m_row[R], reset, a2[R], FAR, ALU.add, ALU.max).then_inc(dve_own, c.up(dve_own))
            dve.wait_ge(dve_own, c.all(dve_own))
            v.tensor_tensor(em_row[R], b_row[R], m_row[R], ALU.add).then_inc(dve_own, c.up(dve_own))
            op = v.tensor_scalar(wu_row[R, 0:SEQ], a_row[R, 0:SEQ], m_row[R, SEQ - 1:SEQ], None, ALU.subtract)
            op.then_inc(dve_own, c.up(dve_own))
            m_last = frames(m_row)[:, :, STEP - 1:STEP]
            op = v.tensor_tensor(frames(wu_row), frames(a_row), m_last.to_broadcast([HEADS, STREAMS, STEP]),
                                 ALU.subtract)
            op.then_inc(dve_own, c.up(dve_own))
            v.tensor_tensor(own_tiles(wi_row[R]), m0.unsqueeze(2).to_broadcast([HEADS, STREAMS, STEP]),
                                frames(m_row), ALU.subtract).then_inc(dve_own, c.up(dve_own))
            op = v.tensor_tensor(m_out[R, 0:1], b_row[R, SEQ - 1:SEQ], m_row[R, SEQ - 1:SEQ], ALU.add)
            op.then_inc(dve_own, c.up(dve_own))
            op = v.tensor_tensor(m_out[R, 1:1 + STREAMS], frames(b_row)[:, :, STEP - 1],
                                 frames(m_row)[:, :, STEP - 1], ALU.add)
            op.then_inc(dve_own, c.up(dve_own))
            op = v.tensor_tensor(dec_row[R, 0:STREAMS], m0, frames(m_row)[:, :, STEP - 1], ALU.subtract)
            op.then_inc(exp_args, c.up(exp_args))
            dve.wait_ge(exp_rows, c.next(exp_rows))
            onehot = rowc[R, R_ONEH:R_ONEH + HEADS]
            op = v.tensor_tensor(decsel[R], dec_row[R, 0:STREAMS].unsqueeze(1).to_broadcast([HEADS, HEADS, STREAMS]),
                                            onehot.unsqueeze(2).to_broadcast([HEADS, HEADS, STREAMS]), ALU.mult)
            op.then_inc(sel_ready, c.up(sel_ready))
            dve.wait_ge(G.bfill[1], c.next(G.bfill[1]))
            op = v.tensor_copy(decb.rearrange("p a b -> p (a b)"), bank[1][:, 0:HEADS * STREAMS])
            op.then_inc(cols_ready, c.up(cols_ready))
            dve.wait_ge(G.bfill[0], c.next(G.bfill[0]))
            op = v.tensor_copy(cols.rearrange("p a b c -> p (a b c)"), bank[0][:, 0:3 * TT * HEADS])
            op.then_inc(G.bfree[0], c.up(G.bfree[0]))
            dve.wait_ge(G.bfree[0], c.all(G.bfree[0]))
            dve.wait_ge(cols_ready, c.all(cols_ready))
            dve.wait_ge(dve_own, c.all(dve_own))

            def stage_b(h):
                own_head = rowc[R, bass.ds(h + R_ONEH, 1)]
                if (due := c.all(B.fill[0])) is not None:
                    dve.wait_ge(B.fill[0], due)
                v.tensor_scalar(msel[R], m_row[R], own_head, None, ALU.mult).then_inc(dve_own, c.up(dve_own))
                v.tensor_scalar(wisel[R], wi_row[R], own_head, None, ALU.mult).then_inc(sel_ready, c.up(sel_ready))

                if (due := c.all(y_ready)) is not None:
                    dve.wait_ge(y_ready, due)

                def split(src, part):
                    flat3 = [part[:, n, :].rearrange("p (a b) -> p a b", b=P) for n in range(3)]
                    r = rest.rearrange("p (a b) -> p a b", b=P)
                    v.tensor_copy(flat3[0], src).then_inc(dve_own, c.up(dve_own))
                    dve.wait_ge(dve_own, c.all(dve_own))
                    v.tensor_tensor(r, src, flat3[0], ALU.subtract).then_inc(dve_own, c.up(dve_own))
                    dve.wait_ge(dve_own, c.all(dve_own))
                    v.tensor_copy(flat3[1], r).then_inc(dve_own, c.up(dve_own))
                    dve.wait_ge(dve_own, c.all(dve_own))
                    v.tensor_tensor(flat3[2], r, flat3[1], ALU.subtract).then_inc(parts_ready, c.up(parts_ready))
                    dve.wait_ge(parts_ready, c.all(parts_ready))

                for q in range(KH):
                    dve.wait_ge(B.fill[1], c.next(B.fill[1]))
                    v.tensor_copy(two(k_t[:, q, :]), halves(work[1])).then_inc(B.free[1], c.up(B.free[1]))
                    if q == 1:
                        dve.wait_ge(hv_in, c.next(hv_in, step=16))
                        if (due := c.all(parts_out, step=16)) is not None:
                            dve.wait_ge(parts_out, due)
                        split(vh[:, :, NP, :], v_part)
                        c.skip(parts_out, 2, 16)
                dve.wait_ge(kw_ready, c.next(kw_ready))
                split(kh[:, :, NP, :], k_part)
                c.skip(kw_ready)
                dve.wait_ge(B.fill[1], c.next(B.fill[1]))
                op = v.tensor_tensor(wpar, parity, work[1][:, 0:P].unsqueeze(1).to_broadcast([P, 2, P]), ALU.mult)
                op.then_inc(B.free[1], c.up(B.free[1]))
                dve.wait_ge(B.free[1], c.all(B.free[1]))
                c.skip(B.fill[0], KH)
                dve.wait_ge(B.fill[0], c.next(B.fill[0]))
                for par in range(2):
                    raised = qm_ready if par else dve_own
                    op = v.tensor_tensor(qm[:, :, par, :], q_t[:, :, SEQ:T],
                                         wpar[:, par, :].unsqueeze(1).to_broadcast([P, KH, P]), ALU.mult)
                    op.then_inc(raised, c.up(raised))
                for t in range(TT):
                    raised = dmax_ready if t == TT - 1 else dve_own
                    op = v.scalar_tensor_tensor(pt[:, OFF[t]:OFF[t] + P], work[0][:, t * P:(t + 1) * P],
                                                cols[:, 0, t, bass.ds(h, 1)], later[:, t // NP, :], ALU.max, ALU.add)
                    op.then_inc(raised, c.up(raised))
                c.skip(B.free[0], KH)
                dve.wait_ge(B.free[0], c.next(B.free[0]))
                for t in range(TT):
                    b = t % 2
                    dve.wait_ge(B.bfill[b], c.next(B.bfill[b]))
                    own_cols = pt[:, OFF[t]:OFF[t] + WID[t]]
                    op = v.tensor_tensor(own_cols, bank[b][:, 0:WID[t]], own_cols, ALU.mult)
                    op.then_inc(B.bfree[b], c.up(B.bfree[b]))

                def statistics(t):
                    src = bank[2 if t < NP else 3]
                    den = small[:, S_DEN + t:S_DEN + t + 1]
                    if t < NP:
                        dve.wait_ge(B.bfill[2], c.next(B.bfill[2]))
                    else:
                        dve.wait_ge(B.bfill[3], c.next(B.bfill[3]))
                        op = v.tensor_tensor(nqm, small[:, S_NQ:S_NQ + STREAMS], bmask, ALU.mult)
                        op.then_inc(dve_own, c.up(dve_own))
                        dve.wait_ge(dve_own, c.all(dve_own))
                        v.reduce_sum(tiny[:, 6:7], nqm, AX_X).then_inc(dve_own, c.up(dve_own))
                        dve.wait_ge(dve_own, c.all(dve_own))
                        v.tensor_tensor(tiny[:, 7:8], tiny[:, 6:7], den, ALU.add).then_inc(dve_own, c.up(dve_own))
                        dve.wait_ge(dve_own, c.all(dve_own))
                        den = tiny[:, 7:8]
                    v.tensor_copy(tiny[:, 0:1], den).then_inc(dve_own, c.up(dve_own))
                    v.bn_stats(st6, src[:, :]).then_inc(dve_own, c.up(dve_own))
                    dve.wait_ge(dve_own, c.all(dve_own))
                    op = v.scalar_tensor_tensor(tiny[:, 1:2], tiny[:, 0:1], -1.0, tiny[:, 0:1], ALU.mult, ALU.max)
                    op.then_inc(dve_own, c.up(dve_own))
                    v.bn_aggr(mv, st6).then_inc(dve_own, c.up(dve_own))
                    dve.wait_ge(dve_own, c.all(dve_own))
                    op = v.tensor_tensor(tiny[:, 1:2], tiny[:, 1:2], cols[:, 1, t, bass.ds(h, 1)], ALU.max)
                    op.then_inc(dve_own, c.up(dve_own))
                    dve.wait_ge(dve_own, c.all(dve_own))
                    v.reciprocal(tiny[:, 2:3], tiny[:, 1:2]).then_inc(dve_own, c.up(dve_own))
                    dve.wait_ge(dve_own, c.all(dve_own))
                    op = v.tensor_scalar(tiny[:, 4:5], mv[:, 1:2], tiny[:, 2:3], None, ALU.mult)
                    op.then_inc(dve_own, c.up(dve_own))
                    dve.wait_ge(dve_own, c.all(dve_own))
                    op = v.tensor_scalar(tiny[:, 3:4], tiny[:, 4:5], tiny[:, 2:3], EPS, ALU.mult, ALU.add)
                    op.then_inc(var_ready, c.up(var_ready))

                def normalise(t):
                    b = 2 if t < NP else 3
                    dve.wait_ge(pow_ready, c.next(pow_ready))
                    op = v.tensor_scalar(hn, bank[b][:, :], mv[:, 0:1], tiny[:, 5:6], ALU.subtract, ALU.mult)
                    op.then_inc(B.bfree[b], c.up(B.bfree[b]))

                def stream(b):
                    s = b % CS
                    for q in range(KH):
                        dve.wait_ge(B.bfill[q % 2], c.next(B.bfill[q % 2]))
                        op = v.scalar_tensor_tensor(
                            ct[s][:, q, :], ct[s][:, q, :], decb[:, h, b:b + 1], bank[q % 2][:, :], ALU.mult, ALU.add)
                        op.then_inc(B.bfree[q % 2], c.up(B.bfree[q % 2]))

                statistics(0)
                stream(0)
                stream(1)
                normalise(0)
                statistics(1)
                stream(2)
                normalise(1)
                statistics(2)
                stream(3)
                normalise(2)
                statistics(3)
                stream(4)
                normalise(3)
                stream(5)
                stream(6)
                stream(7)
                for q in range(2):
                    c.skip(B.bfill[q], 2)
                    c.skip(B.bfree[q], 2)
                statistics(NP)
                normalise(NP)
                op = v.tensor_tensor(n_t[:, h], n_t[:, h],
                                     decb[:, h].unsqueeze(1).to_broadcast([P, KH, STREAMS]), ALU.mult)
                op.then_inc(dve_own, c.up(dve_own))
                dve.wait_ge(dve_own, c.all(dve_own))
                op = v.tensor_tensor(n_t[:, h], n_t[:, h],
                                     small[:, S_NS:S_NS + KH * STREAMS].rearrange("p (a b) -> p a b", b=STREAMS), ALU.add)
                op.then_inc(dve_own, c.up(dve_own))
                v.tensor_copy(p_n[:, h], small[:, S_NP:S_NP + KH]).then_inc(B.free[1], c.up(B.free[1]))
                c.skip(B.free[0], TT - 1)
                dve.wait_ge(B.free[0], c.next(B.free[0]))
                dve.wait_ge(hz_in, c.next(hz_in, step=16))
                c.skip(B.fill[0], TT)
                for q in range(KH):
                    n = h * KH + q
                    v.scalar_tensor_tensor(h_t[:, q, :], xc[:, n, :], vec[:, bass.ds(n + V_SK, 1)], h_t[:, q, :],
                                               ALU.mult, ALU.add).then_inc(dve_own, c.up(dve_own))
                dve.wait_ge(dve_own, c.all(dve_own))
                v.tensor_tensor(xc[:, bass.ts(h, KH), :], h_t, zh, ALU.mult).then_inc(y_ready, c.up(y_ready))
            c.rounds(HEADS, stage_b)
            leave(c, 2)

            dve.wait_ge(x1_in, c.next(x1_in, step=16))

            def stage_c(m):
                for s in range(2):
                    dve.wait_ge(C.fill[s], c.next(C.fill[s]))
                    x = two(x1[:, m * 2 + s, :])
                    v.tensor_tensor(x, x, halves(work[s]), ALU.add).then_inc(C.free[s], c.up(C.free[s]))
            c.rounds(KD // 2, stage_c)

            invert(rstd[:])
            for k in range(KD):
                scale_norm(xk, x1, V_KN, rstd[:], k, normed)
            for k in range(KD):
                scale_norm(xb, x1, V_BN, rstd[:], k, normed)
            invert(lrstd)
            for k in range(RT):
                scale_norm(ckv, ckv, V_LN, lrstd, k, lat_ready if k == RT - 1 else dve_own)
            dve.wait_ge(late_in, c.all(late_in, ahead=5, step=16))

            def rotate(outs, done, free):
                v.tensor_tensor(two(rot), halves(work[1]), two(rope_s), ALU.mult).then_inc(dve_own, c.up(dve_own))
                v.tensor_tensor(pe_raw, pe_raw, rope_c, ALU.mult).then_inc(free, c.up(free))
                dve.wait_ge(dve_own, c.all(dve_own))
                dve.wait_ge(free, c.all(free))
                for m, (rows, out) in enumerate(outs):
                    raised = done if m == len(outs) - 1 else dve_own
                    v.tensor_tensor(out[rows], pe_raw[rows], rot[rows], ALU.add).then_inc(raised, c.up(raised))

            dve.wait_ge(rope_mm, c.next(rope_mm))
            v.tensor_tensor(two(rot), halves(work[1]), two(rope_s), ALU.mult).then_inc(dve_own, c.up(dve_own))
            v.tensor_tensor(pe_raw, pe_raw, rope_c, ALU.mult).then_inc(dve_own, c.up(dve_own))
            dve.wait_ge(dve_own, c.all(dve_own))
            v.tensor_tensor(kpe, pe_raw, rot, ALU.add).then_inc(kpe_ready, c.up(kpe_ready))
            invert(qrstd)
            for k in range(QT):
                scale_norm(cq, cq, V_QN, qrstd, k, dve_own)
            leave(c, 3)

            def row_max(bufs, b, n):
                dve.wait_ge(bufs.bfill[b], c.next(bufs.bfill[b]))
                v.reduce_max(mx[:, b:b + 1], bank[b][:, 0:n], AX_X).then_inc(dve_own, c.up(dve_own))
                dve.wait_ge(dve_own, c.all(dve_own))
                op = v.tensor_scalar(nmx[:, b:b + 1], mx[:, b:b + 1], -ASCALE, None, ALU.mult)
                op.then_inc(max_ready, c.up(max_ready))

            def probabilities(bufs, b, rows):
                dve.wait_ge(bufs.bfree[b], c.next(bufs.bfree[b]))
                v.reciprocal(rinv[:, b:b + 1], rsum[:, b:b + 1]).then_inc(dve_own, c.up(dve_own))
                dve.wait_ge(dve_own, c.all(dve_own))
                v.tensor_scalar(rows, rows, rinv[:, b:b + 1], None, ALU.mult).then_inc(prob_ready, c.up(prob_ready))

            v.memset(qz, 0.0).then_inc(dve_own, c.up(dve_own))
            dve.wait_ge(dve_own, c.all(dve_own))

            def stage_e(p):
                c.skip(E.fill[1])
                c.skip(E.free[1])
                for a in range(2):
                    w = 1 - a
                    if a:
                        c.skip(E.fill[0], 2)
                    dve.wait_ge(E.fill[w], c.next(E.fill[w]))
                    v.tensor_copy(kn[a], work[w][:, 0:SEQ]).then_inc(E.free[w], c.up(E.free[w]))
                dve.wait_ge(E.fill[1], c.next(E.fill[1]))
                v.tensor_tensor(pe_raw, pe_raw, rope_c, ALU.mult).then_inc(dve_own, c.up(dve_own))
                v.tensor_tensor(two(rot), halves(work[1]), two(rope_s), ALU.mult).then_inc(E.free[1], c.up(E.free[1]))
                dve.wait_ge(dve_own, c.all(dve_own))
                dve.wait_ge(E.free[1], c.all(E.free[1]))
                for a, rows in enumerate((slice(0, ROPE), slice(ROPE, P))):
                    raised = qz_ready if a else dve_own
                    v.tensor_tensor(qz[rows, a, :], pe_raw[rows], rot[rows], ALU.add).then_inc(raised, c.up(raised))
                dve.wait_ge(qz_ready, c.all(qz_ready))
                dve.wait_ge(dve_own, c.all(dve_own))
                for a in range(2):
                    op = v.tensor_copy(qs[:, 2, :, p * 2 + a, :], own_tiles(qz[:, a, SEQ:T]))
                    op.then_inc(dve_own, c.up(dve_own))
                dve.wait_ge(E.fill[1], c.next(E.fill[1]))
                for n in range(4):
                    a, r = divmod(n, RT)
                    raised = (pair_done, dve_own, dve_own, E.free[1])[n]
                    op = v.tensor_copy(qs[:, r, :, p * 2 + a, :], own_tiles(work[1][:, n * P:(n + 1) * P]))
                    op.then_inc(raised, c.up(raised))

                def outputs(a):
                    dve.wait_ge(E.fill[a], c.next(E.fill[a]))
                    h = p * 2 + a
                    op = v.tensor_tensor(og[:, h, 0:SEQ], work[a][:, 0:SEQ], gate[:, h, 0:SEQ], ALU.mult)
                    op.then_inc(E.free[a], c.up(E.free[a]))

                for u in range(2 * NP):
                    row_max(E, u % 2, (u % NP + 1) * P)
                    if u == 0:
                        c.skip(E.fill[0])
                    else:
                        probabilities(E, (u - 1) % 2, pexp[(u - 1) % 2][:, 0:((u - 1) % NP + 1) * P])
                    if u == NP:
                        outputs(0)
                probabilities(E, 1, pexp[1])
                outputs(1)
            c.rounds(PAIRS, stage_e)
            leave(c, 4)

            def stage_f(m):
                for s in range(2):
                    row_max(F, s, 3 * P)
                for s in range(2):
                    probabilities(F, s, pexp_f[s])
                for s in range(2):
                    dve.wait_ge(F.fill[s], c.next(F.fill[s]))
                    op = v.tensor_copy(osT[:, :, :, m * 2 + s, :],
                                                  work[s][:, 0:LAT].rearrange("p (a h t) -> p a h t", a=RT, t=STEP))
                    op.then_inc(F.free[s], c.up(F.free[s]))
            c.rounds(STREAMS // 2, stage_f)
            for g in range(2):
                dve.wait_ge(H.bfill[g], c.next(H.bfill[g]))
                tiles = slice(4 * g, 4 * g + 4)
                op = v.tensor_tensor(og[:, tiles, SEQ:T], bank[g][:, :].rearrange("p (a b) -> p a b", b=P),
                                                 gate[:, tiles, SEQ:T], ALU.mult)
                op.then_inc(H.bfree[g], c.up(H.bfree[g]))

            def stage_h(m):
                for r in range(SLOTS):
                    dve.wait_ge(H.fill[r % 2], c.next(H.fill[r % 2]))
                    x = two(x1[:, m * SLOTS + r, :])
                    v.tensor_tensor(x, x, halves(work[r % 2]), ALU.add).then_inc(H.free[r % 2], c.up(H.free[r % 2]))
            c.rounds(2, stage_h)
            invert(rstd[:])
            for k in range(KD):
                scale_norm(x1, x1, V_FN, rstd[:], k, y_out)

        @block.gpsimd
        def _(pool):
            c = Counts(pool)
            g = nc.gpsimd
            g.memset(eps_t[:], EPS).then_inc(pool_own, c.up(pool_own))
            g.memset(ones_f[:], 1.0).then_inc(ones_ready, c.up(ones_ready))

            def stage_a(j):
                for s in range(2):
                    n = j * 2 + s
                    pool.wait_ge(tap0, c.next(tap0))
                    g.tensor_copy(tails[:, n, 0, :], xin[s][:, SEQ:PROMPT_X]).then_inc(pool_own, c.up(pool_own))
                    op = g.tensor_copy(tails[:, n, 1:1 + STREAMS, :], x_streams(s, STEP, HIST))
                    op.then_inc(tail_kept, c.up(tail_kept))
                    pool.wait_ge(xcs_ready, c.next(xcs_ready))
                    g.tensor_copy(xc[:, n, :], xcs[s]).then_inc(xc_kept, c.up(xc_kept))
            c.rounds(NI // 2, stage_a)
            leave(c, 1)

            def head_basis(h):
                for n, (out, w) in enumerate(((bdq, wq_c), (bdk, wk_c))):
                    for q in range(KH):
                        raised = bd_ready if n == 1 and q == KH - 1 else pool_own
                        op = g.tensor_tensor(out[:, q, :].rearrange("p (a b) -> p a b", b=4), bdmask[:],
                                             w[:, h * KH + q, :].unsqueeze(1).to_broadcast([P, 32, 4]), ALU.mult)
                        op.then_inc(raised, c.up(raised))

            head_basis(0)

            def stage_b(h):
                def inverse_root():
                    pool.wait_ge(var_ready, c.next(var_ready))
                    g.tensor_tensor(tiny[:, 4:5], tiny[:, 3:4], half_neg, ALU.pow).then_inc(pool_own, c.up(pool_own))
                    pool.wait_ge(pool_own, c.all(pool_own))
                    op = g.tensor_tensor(tiny[:, 5:6], tiny[:, 4:5], tiny[:, 2:3], ALU.mult)
                    op.then_inc(pow_ready, c.up(pow_ready))

                pool.wait_ge(kw_ready, c.next(kw_ready))
                pool.wait_ge(kw_ready, c.next(kw_ready))
                g.tensor_tensor(kwsum, kh[:, :, 0, :], kh[:, :, 1, :], ALU.add).then_inc(pool_own, c.up(pool_own))
                pool.wait_ge(pool_own, c.all(pool_own))
                inverse_root()
                g.tensor_tensor(kwsum, kwsum, kh[:, :, 2, :], ALU.add).then_inc(pool_own, c.up(pool_own))
                pool.wait_ge(pool_own, c.all(pool_own))
                inverse_root()
                g.tensor_tensor(kwsum, kwsum, kh[:, :, 3, :], ALU.add).then_inc(kwsum_ready, c.up(kwsum_ready))
                inverse_root()
                pool.wait_ge(B.fill[1], c.all(B.fill[1], ahead=4))
                c.skip(B.fill[1], 5)
                head_basis(h + 1)
                inverse_root()
                inverse_root()
            c.rounds(HEADS, stage_b)
            leave(c, 2)
            pool.wait_ge(late_in, c.all(late_in, ahead=5, step=16))
            for dst, first in ((mask_l, 0), (mask_r, P)):
                g.tensor_copy(dst[0:1], mask_rows[0:1, first:first + P]).then_inc(pool_own, c.up(pool_own))
            op = g.tensor_copy(own_keys[0:1].rearrange("p a b -> p (a b)"), mask_rows[0:1, 2 * P:])
            op.then_inc(pool_own, c.up(pool_own))
            g.memset(ones16[0:1], 1.0).then_inc(pool_own, c.up(pool_own))
            leave(c, 3)
            leave(c, 4)


def _tiles(a, k):
    return a.reshape(k, P, -1).transpose(1, 0, 2)


def _lay_out(np, x):
    f = np.float32
    at = lambda name: np.asarray(x[name])
    tokens = np.concatenate([at("x_prompt").reshape(SEQ, D), at("x_sample").reshape(STREAMS * STEP, D)])
    col = lambda a: np.asarray(a).reshape(-1, P).T

    def blocks(w):
        return w.reshape(w.shape[0] // P, P, w.shape[1] // P, P).transpose(2, 1, 0, 3)

    w_in = blocks(at("a_w_in")[0])
    w_out = blocks(at("a_w_out")[0])
    dkv = at("kv_w_dkv")
    dkv = blocks(np.concatenate([dkv, dkv[:, LAT:]], axis=1))
    b_in, b_out = blocks(at("b_w_in")[0]), blocks(at("b_w_out")[0])
    stream = np.concatenate(
        [np.stack([w_in[:NI], w_in[NI:]], axis=1).reshape(2 * NI, P, KD, P),
         w_out.reshape(KD, P, 2, KD, P).transpose(0, 2, 1, 3, 4).reshape(2 * KD, P, KD, P), dkv, b_in, b_out])
    conv_w = at("a_conv_w")[0].reshape(TAPS, NI, P).transpose(2, 1, 0).reshape(P, NI * TAPS)
    vec = np.concatenate([conv_w, col(at("a_conv_b")[0]), col(at("a_outnorm_w")[0]), col(at("a_skip")[0]),
                          col(at("a_norm_w")[0]), col(at("kv_norm_w")), col(at("b_norm_w")[0]),
                          col(at("final_norm_w")), col(at("kv_latent_norm_w")), col(at("b_q_norm_w")[0])], axis=1)
    compact = lambda name: at(name)[0].reshape(NI, P, 4).transpose(1, 0, 2)
    padded = lambda a: np.concatenate([a, np.zeros((P, KH, 4), f)], axis=1)
    gw = at("a_w_gates")[0].reshape(3, NI, 32, 1, 4, G8)
    gqkv = np.broadcast_to(gw, (3, NI, 32, 4, 4, G8)).reshape(3, NI, P, 4, G8).transpose(2, 0, 1, 3, 4)
    hist = at("state_mlstm_conv")[0].reshape(STREAMS, HIST, NI, P).transpose(3, 2, 0, 1)
    keep, reset = np.ones((HEADS, T), f), np.zeros((HEADS, T), f)
    starts = [0] + list(range(SEQ, T, STEP))
    keep[:, starts], reset[:, starts] = 0.0, FAR
    bg = at("a_b_gates")[0].reshape(2, HEADS)
    rows = np.concatenate([bg.T, np.zeros((HEADS, 1), f), at("state_mlstm_m")[0].T, keep, reset,
                           np.eye(HEADS, dtype=f)], axis=1)
    token = np.arange(P)
    stream_of = token // STEP
    after = token[:, None] > token[None, :]
    other = stream_of[:, None] != stream_of[None, :]
    later = np.stack([after, after | other], axis=1).astype(f) * f(-FAR)
    parity = np.broadcast_to((stream_of % 2)[None, None, :] == np.arange(2)[None, :, None], (P, 2, P)).astype(f)
    bmask = (stream_of[:, None] == np.arange(STREAMS)[None, :]).astype(f)
    c0 = at("state_mlstm_C")[0].transpose(1, 0, 3, 2).reshape(HEADS * STREAMS, KH, P, HD).transpose(0, 2, 1, 3)
    n0 = at("state_mlstm_n")[0].reshape(STREAMS, HEADS, KH, P).transpose(3, 1, 2, 0)
    half = ROPE // 2
    pos = np.concatenate([np.arange(SEQ), PAST + np.tile(np.arange(STEP), STREAMS)]).astype(f)
    inv = f(10000.0) ** (-np.arange(half, dtype=f) / f(half))
    ang = (pos[None, :] * inv[:, None]).astype(f)
    cos = np.tile(np.cos(ang), (4, 1)).astype(f)
    sin = np.tile(np.concatenate([-np.sin(ang), np.sin(ang)]), (2, 1)).astype(f)
    swap = np.zeros((P, P), f)
    swap[(token // ROPE) * ROPE + (token + half) % ROPE, token] = 1.0
    uq = at("b_w_uq")[0].reshape(QT, P, PAIRS, 2, P + ROPE)
    nope = uq[..., :P].transpose(2, 1, 3, 0, 4)
    rope = uq[..., P:].transpose(2, 1, 0, 3, 4).reshape(PAIRS, P, 1, QT, P)
    uk = at("kv_w_uk")
    uk_a = uk.reshape(RT, P, PAIRS, 2, P).transpose(2, 1, 3, 0, 4)
    uk_t = uk.transpose(2, 1, 0).reshape(P, PAIRS, 2, RT, P).transpose(1, 0, 2, 3, 4)
    pairw = np.concatenate([np.concatenate([nope, rope], axis=2).reshape(PAIRS, P, 9, P),
                            uk_a.reshape(PAIRS, P, 4, P), uk_t.reshape(PAIRS, P, 4, P)], axis=2)
    ckv_c, kpe_c = at("cache_mla_ckv"), at("cache_mla_kpe")
    keys_t = ckv_c.transpose(0, 2, 1).reshape(STREAMS, RT, P, 2, P).transpose(0, 2, 1, 3, 4).reshape(STREAMS, P, 4, P)
    kpe_t = np.concatenate([kpe_c, kpe_c], axis=2).transpose(0, 2, 1).reshape(STREAMS, P, 2, P)
    by_token = ckv_c.reshape(STREAMS, 2, P, RT, P).transpose(0, 2, 1, 3, 4).reshape(STREAMS, P, 4, P)
    keys = np.concatenate([keys_t, kpe_t, by_token], axis=2)
    own_keys = np.where(stream_of[None, :] == np.arange(STREAMS)[:, None], 0.0, FAR)
    masks = np.concatenate([token < 64, np.where(token < 64, 0.0, FAR), own_keys.reshape(-1)]).astype(f)[None]
    return {
        "x": _tiles(tokens.T, KD), "stream": stream, "vec": vec, "wq": padded(compact("a_w_q")),
        "wk": padded(compact("a_w_k")), "wv": compact("a_w_v"), "gqkv": gqkv, "hist": hist, "rows": rows,
        "later": later, "parity": parity, "bmask": bmask, "c0": c0, "n0": n0, "cos": cos, "sin": sin, "swap": swap,
        "uv": _tiles(at("kv_w_uv").reshape(LAT, AH * P), RT), "pairw": pairw, "keys": keys, "masks": masks, "ident": np.eye(P, dtype=f),
        "bdmask": (np.arange(32)[None, :, None] == (token // 4)[:, None, None]).astype(f) * np.ones((1, 1, 4), f),
    }


_OUT = {"y": (P, KD, T), "ckv": (P, RT, T), "kpe": (ROPE, T), "conv": (P, NI, 1 + STREAMS, HIST),
        "s_c": (HEADS * STREAMS, P, KH, HD), "p_c": (HEADS * KH, P, HD), "s_n": (P, HEADS, KH, STREAMS),
        "p_n": (P, HEADS, KH), "m": (HEADS, 1 + STREAMS)}


def kernel(**inputs):
    import numpy as np
    import concourse.bacc as bacc
    from concourse.bass_utils import run_bass_kernel_spmd

    nc = bacc.Bacc("TRN2", target_bir_lowering=False, num_devices=1)
    arrays = {f"in_{n}": np.ascontiguousarray(a) for n, a in _lay_out(np, inputs).items()}
    i = {n[3:]: nc.dram_tensor(n, a.shape, mybir.dt.from_np(a.dtype), kind="ExternalInput").ap()
         for n, a in arrays.items()}
    o = {n: nc.dram_tensor(f"out_{n}", s, F32, kind="ExternalOutput").ap() for n, s in _OUT.items()}
    program(nc, i, o)
    r = run_bass_kernel_spmd(nc, [arrays], core_ids=[0]).results[0]
    y, ckv, kpe, conv, s_c, p_c, s_n, p_n, m = (np.asarray(r[f"out_{n}"]) for n in
                                                ("y", "ckv", "kpe", "conv", "s_c", "p_c", "s_n", "p_n", "m"))
    y = y.transpose(2, 1, 0).reshape(T, D)
    ckv = ckv.transpose(2, 1, 0).reshape(T, LAT)
    kpe = kpe.T
    conv = conv.transpose(2, 3, 1, 0).reshape(1 + STREAMS, HIST, INNER)
    s_c = s_c.reshape(HEADS, STREAMS, P, KH, HD).transpose(1, 0, 4, 3, 2).reshape(1, STREAMS, HEADS, HD, HD)
    p_c = p_c.reshape(HEADS, HD, HD).transpose(0, 2, 1)[None, None]
    s_n = s_n.transpose(3, 1, 2, 0).reshape(1, STREAMS, HEADS, HD)
    p_n = p_n.transpose(1, 2, 0).reshape(1, 1, HEADS, HD)
    split = lambda a, n: (a[:SEQ].reshape(1, SEQ, n), a[SEQ:].reshape(STREAMS, STEP, n))
    (y_p, y_s), (ckv_p, ckv_s), (kpe_p, kpe_s) = split(y, D), split(ckv, LAT), split(kpe, ROPE)
    c = np.ascontiguousarray
    return tuple(c(a) for a in (
        y_p, y_s, p_c, p_n, m.T[None, 0:1], conv[None, 0:1], ckv_p, kpe_p,
        s_c, s_n, m.T[None, 1:], conv[None, 1:], ckv_s, kpe_s))
```
